# Optimizing a Trainium2 kernel written in Bass

```python
import math
import jax, jax.numpy as jnp
from jax import lax
import numpy as np

D_MODEL = 1024
BATCH = 1
SEQ = 512
DEPTH = 2

CTX_LEN = 256
GRID_W = 64

DEEPNORM_ALPHA = (2.0 * DEPTH) ** 0.25
DEEPNORM_BETA = (8.0 * DEPTH) ** -0.25
LN_EPS = 1e-6

SSD_HEAD_DIM = 64
D_SSD = D_MODEL
SSD_HEADS = D_SSD // SSD_HEAD_DIM
SSD_GROUPS = 4
SSD_HPG = SSD_HEADS // SSD_GROUPS
SSD_STATE = 128
SSD_CHUNK = 128
CONV_W = 5
CONV_CH = D_SSD + 2 * SSD_GROUPS * SSD_STATE

POOL_GROUPS = 4
POOL_CH = D_MODEL // 8
POOL_WINDOWS = (2, 4, 8, 16)
POOL_OUT = D_MODEL // POOL_GROUPS

PEER_HEADS = 8
N_KEYS = 128
N_EXPERTS = N_KEYS * N_KEYS
PEER_TOPK = 16
PEER_QDIM = 256
D_HALF = PEER_QDIM // 2
PEER_BLOCK = 128

COL_B = D_SSD
COL_C = COL_B + SSD_GROUPS * SSD_STATE
COL_DTF = COL_C + SSD_GROUPS * SSD_STATE
COL_DTB = COL_DTF + SSD_HEADS
SCAN_COLS = COL_DTB + SSD_HEADS
COL_Z = SCAN_COLS
COL_POOL = COL_Z + D_SSD
COL_GP = COL_POOL + POOL_GROUPS * POOL_CH
COL_GS = COL_GP + D_MODEL
W_IN_COLS = COL_GS + D_MODEL

kernel_name = "hybrid_pool_ssd_peer_diffusion_block"

def layer_norm(x, g, b):
    xf = x.astype(jnp.float32)
    mu = jnp.mean(xf, axis=-1, keepdims=True)
    var = jnp.mean(jnp.square(xf - mu), axis=-1, keepdims=True)
    return ((xf - mu) * lax.rsqrt(var + LN_EPS) * g + b).astype(x.dtype)

def depthwise_conv(u, w, b):
    out = lax.conv_general_dilated(
        u, w[:, None, :], window_strides=(1,),
        padding=[(CONV_W // 2, CONV_W // 2)],
        dimension_numbers=("NWC", "WIO", "NWC"),
        feature_group_count=u.shape[-1])
    return out + b

def box_mean(u, w):
    L = u.shape[1]
    lo_off = w // 2
    hi_off = w - 1 - lo_off
    uf = u.astype(jnp.float32)
    cs = jnp.concatenate([jnp.zeros_like(uf[:, :1]), jnp.cumsum(uf, axis=1)], axis=1)
    t = jnp.arange(L)
    lo = jnp.maximum(t - lo_off, 0)
    hi = jnp.minimum(t + hi_off, L - 1)
    cnt = (hi - lo + 1).astype(jnp.float32).reshape((1, L) + (1,) * (u.ndim - 2))
    return ((cs[:, hi + 1] - cs[:, lo]) / cnt).astype(u.dtype)

def pool_branch(u, pool_w, pool_scale, on_grid):
    b, L, _ = u.shape
    ug = u.reshape(b, L, POOL_GROUPS, POOL_CH)
    outs = []
    for gi, w in enumerate(POOL_WINDOWS):
        ui = ug[:, :, gi]
        if on_grid:
            rows = L // GRID_W
            grid = box_mean(ui.reshape(b, rows, GRID_W, POOL_CH), w)
            grid = jnp.swapaxes(box_mean(jnp.swapaxes(grid, 1, 2), w), 1, 2)
            pooled = grid.reshape(b, L, POOL_CH)
        else:
            pooled = box_mean(ui, w)
        outs.append(pooled - ui)
    mixed = jnp.stack(outs, axis=2)
    y = jnp.einsum("blgc,gco->blgo", mixed, pool_w).reshape(b, L, D_MODEL)
    return y * pool_scale

def ssd_prepare(proj_scan, conv_w, conv_b):
    b, L, _ = proj_scan.shape
    xbc = jax.nn.silu(depthwise_conv(proj_scan[..., :COL_DTF], conv_w, conv_b))
    xh = xbc[..., :D_SSD].reshape(b, L, SSD_GROUPS, SSD_HPG, SSD_HEAD_DIM)
    bm = xbc[..., COL_B:COL_C].reshape(b, L, SSD_GROUPS, SSD_STATE)
    cm = xbc[..., COL_C:COL_DTF].reshape(b, L, SSD_GROUPS, SSD_STATE)
    dt_f = proj_scan[..., COL_DTF:COL_DTB].reshape(b, L, SSD_GROUPS, SSD_HPG)
    dt_b = proj_scan[..., COL_DTB:SCAN_COLS].reshape(b, L, SSD_GROUPS, SSD_HPG)
    return xh, bm, cm, dt_f, dt_b

def ssd_scan(xh, bm, cm, dt_raw, a_log, dt_bias, h0, reverse, with_output):
    if reverse:
        xh, bm, cm, dt_raw = [jnp.flip(t, 1) for t in (xh, bm, cm, dt_raw)]
    b, L = xh.shape[:2]
    nc = L // SSD_CHUNK
    dt = jax.nn.softplus(dt_raw + dt_bias.reshape(SSD_GROUPS, SSD_HPG))
    a = -jnp.exp(a_log.reshape(SSD_GROUPS, SSD_HPG))
    chunk = lambda t: t.reshape((b, nc, SSD_CHUNK) + t.shape[2:])
    xc, bc, cc, dtc = chunk(xh), chunk(bm), chunk(cm), chunk(dt)
    a_cum = jnp.cumsum(dtc * a, axis=2)
    decay_to_end = jnp.exp(a_cum[:, :, -1:] - a_cum)
    states = jnp.einsum("bcsgn,bcsgrp->bcgrpn", bc, (decay_to_end * dtc)[..., None] * xc)
    chunk_decay = jnp.exp(a_cum[:, :, -1])

    def step(h, inp):
        s, d = inp
        return d[..., None, None] * h + s, h

    h_last, h_in = lax.scan(step, h0, (jnp.moveaxis(states, 1, 0), jnp.moveaxis(chunk_decay, 1, 0)))
    if not with_output:
        return None, h_last
    h_in = jnp.moveaxis(h_in, 0, 1)
    seg = a_cum[:, :, :, None] - a_cum[:, :, None, :]
    lower = (jnp.arange(SSD_CHUNK)[:, None] >= jnp.arange(SSD_CHUNK)[None, :])[None, None, :, :, None, None]
    decay = jnp.exp(jnp.where(lower, seg, -jnp.inf))
    cb = jnp.einsum("bclgn,bcsgn->bclsg", cc, bc)
    wgt = cb[..., None] * decay * dtc[:, :, None]
    y = jnp.einsum("bclsgr,bcsgrp->bclgrp", wgt, xc)
    y = y + jnp.einsum("bclgn,bcgrpn->bclgrp", cc, h_in) * jnp.exp(a_cum)[..., None]
    y = y.reshape(b, L, SSD_GROUPS, SSD_HPG, SSD_HEAD_DIM)
    if reverse:
        y = jnp.flip(y, 1)
    return y, h_last

def bidir_ssd(xh, bm, cm, dt_f, dt_b, a_log, dt_bias, h0_f, h0_b, with_output):
    y_f, h_f = ssd_scan(xh, bm, cm, dt_f, a_log[0], dt_bias[0], h0_f, False, with_output)
    y_b, h_b = ssd_scan(xh, bm, cm, dt_b, a_log[1], dt_bias[1], h0_b, True, with_output)
    y = y_f + y_b if with_output else None
    return y, h_f, h_b

def ssd_finish(y, xh, z, d_skip, norm_g, w_ssd_out):
    b, L = y.shape[:2]
    y = y + d_skip.reshape(SSD_GROUPS, SSD_HPG)[..., None] * xh
    yg = (y.reshape(b, L, D_SSD) * jax.nn.silu(z)).astype(jnp.float32)
    yg = yg.reshape(b, L, SSD_GROUPS, D_SSD // SSD_GROUPS)
    yg = yg * lax.rsqrt(jnp.mean(yg * yg, axis=-1, keepdims=True) + LN_EPS)
    y = (yg.reshape(b, L, D_SSD) * norm_g).astype(z.dtype)
    return y @ w_ssd_out

def mixer_out(proj, y_ssd, xh, d_skip, norm_g, w_ssd_out, pool_w, pool_scale, w_o, on_grid):
    y_pool = pool_branch(proj[..., COL_POOL:COL_GP], pool_w, pool_scale, on_grid)
    y_s = ssd_finish(y_ssd, xh, proj[..., COL_Z:COL_POOL], d_skip, norm_g, w_ssd_out)
    merged = (jax.nn.sigmoid(proj[..., COL_GP:COL_GS]) * y_pool
              + jax.nn.sigmoid(proj[..., COL_GS:W_IN_COLS]) * y_s)
    return merged @ w_o

def peer(h, w_q, sub_keys, u_tab, v_tab):
    b, L, _ = h.shape
    q = (h @ w_q).reshape(b, L, PEER_HEADS, 2, D_HALF)
    scores = jnp.einsum("blhtd,htkd->blhtk", q, sub_keys)
    sv, si = lax.top_k(scores, PEER_TOPK)
    n_cand = PEER_TOPK * PEER_TOPK
    cand_s = (sv[..., 0, :, None] + sv[..., 1, None, :]).reshape(b, L, PEER_HEADS, n_cand)
    cand_i = (si[..., 0, :, None] * N_KEYS + si[..., 1, None, :]).reshape(b, L, PEER_HEADS, n_cand)
    top_s, pos = lax.top_k(cand_s, PEER_TOPK)
    idx = jnp.take_along_axis(cand_i, pos, axis=-1)
    gate = jax.nn.softmax(top_s.astype(jnp.float32), axis=-1).astype(h.dtype)
    n_tok = b * L
    n_sel = PEER_HEADS * PEER_TOPK
    nb = n_tok // PEER_BLOCK
    xb = h.reshape(nb, PEER_BLOCK, D_MODEL)
    ib = idx.reshape(nb, PEER_BLOCK, n_sel)
    gb = gate.reshape(nb, PEER_BLOCK, n_sel)

    def experts(args):
        xt, it, gt = args
        act = jax.nn.gelu(jnp.einsum("tkd,td->tk", u_tab[it], xt))
        return jnp.einsum("tk,tkd->td", gt * act, v_tab[it])

    out = lax.map(experts, (xb, ib, gb))
    return out.reshape(b, L, D_MODEL)

def setup_inputs(seed: int = 0) -> dict:
    key = jax.random.key(seed)
    ks = jax.random.split(key, 24)
    D = D_MODEL
    nrm = lambda k, shape, s: jax.random.normal(k, shape, jnp.float32) * s
    x = nrm(ks[0], (BATCH, SEQ, D), 1.0)
    c = nrm(ks[1], (BATCH, D), 1.0)
    ctx = nrm(ks[2], (BATCH, CTX_LEN, D), 1.0)
    c_ctx = nrm(ks[3], (D,), 1.0)
    w_mod = nrm(ks[4], (DEPTH, D, 6 * D), 0.5 * D ** -0.5)
    b_mod = nrm(ks[5], (DEPTH, 6 * D), 0.01)
    w_in = nrm(ks[6], (DEPTH, D, W_IN_COLS), D ** -0.5)
    conv_w = nrm(ks[7], (DEPTH, CONV_W, CONV_CH), CONV_W ** -0.5)
    conv_b = nrm(ks[8], (DEPTH, CONV_CH), 0.01)
    a_log = jnp.log(jax.random.uniform(ks[9], (DEPTH, 2, SSD_HEADS), jnp.float32, 1.0, 16.0))
    dt0 = jnp.exp(jax.random.uniform(ks[10], (DEPTH, 2, SSD_HEADS), jnp.float32,
                                     math.log(1e-3), math.log(1e-1)))
    dt_bias = dt0 + jnp.log(-jnp.expm1(-dt0))
    d_skip = 1.0 + nrm(ks[11], (DEPTH, SSD_HEADS), 0.1)
    ssd_norm_g = 1.0 + nrm(ks[12], (DEPTH, D_SSD), 0.1)
    w_ssd_out = nrm(ks[13], (DEPTH, D_SSD, D), D_SSD ** -0.5)
    pool_w = nrm(ks[14], (DEPTH, POOL_GROUPS, POOL_CH, POOL_OUT), POOL_CH ** -0.5)
    pool_scale = 1.0 + nrm(ks[15], (DEPTH, D), 0.1)
    w_o = nrm(ks[16], (DEPTH, D, D), DEEPNORM_BETA * D ** -0.5)
    ln_g = 1.0 + nrm(ks[17], (DEPTH, 2, D), 0.1)
    ln_b = nrm(ks[18], (DEPTH, 2, D), 0.01)
    w_q = nrm(ks[19], (DEPTH, D, PEER_HEADS * PEER_QDIM), D ** -0.5)
    sub_keys = nrm(ks[20], (DEPTH, PEER_HEADS, 2, N_KEYS, D_HALF), D_HALF ** -0.5)
    u_tab = nrm(ks[21], (DEPTH, N_EXPERTS, D), D ** -0.5)
    v_tab = nrm(ks[22], (DEPTH, N_EXPERTS, D), DEEPNORM_BETA)
    return {"x": x, "c": c, "ctx": ctx, "c_ctx": c_ctx, "w_mod": w_mod, "b_mod": b_mod,
            "w_in": w_in, "conv_w": conv_w, "conv_b": conv_b, "a_log": a_log, "dt_bias": dt_bias,
            "d_skip": d_skip, "ssd_norm_g": ssd_norm_g, "w_ssd_out": w_ssd_out, "pool_w": pool_w,
            "pool_scale": pool_scale, "w_o": w_o, "ln_g": ln_g, "ln_b": ln_b, "w_q": w_q,
            "sub_keys": sub_keys, "u_tab": u_tab, "v_tab": v_tab}

def reference(x, c, ctx, c_ctx, w_mod, b_mod, w_in, conv_w, conv_b, a_log, dt_bias, d_skip,
              ssd_norm_g, w_ssd_out, pool_w, pool_scale, w_o, ln_g, ln_b, w_q, sub_keys, u_tab, v_tab):
    D = D_MODEL
    silu_c = jax.nn.silu(c)
    silu_cc = jax.nn.silu(c_ctx)
    for l in range(DEPTH):
        last = l == DEPTH - 1
        mod = (silu_c @ w_mod[l] + b_mod[l])[:, None, :]
        sh1, sc1, g1, sh2, sc2, g2 = jnp.split(mod, 6, axis=-1)
        n_ctx_cols = 2 * D if last else 6 * D
        mod_c = silu_cc @ w_mod[l][:, :n_ctx_cols] + b_mod[l][:n_ctx_cols]
        mods_c = jnp.split(mod_c, n_ctx_cols // D)

        hc = ctx * (1 + mods_c[1]) + mods_c[0]
        proj_c = hc @ (w_in[l][:, :SCAN_COLS] if last else w_in[l])
        xh_c, b_c, c_c, dtf_c, dtb_c = ssd_prepare(proj_c[..., :SCAN_COLS], conv_w[l], conv_b[l])
        h0 = jnp.zeros((ctx.shape[0], SSD_GROUPS, SSD_HPG, SSD_HEAD_DIM, SSD_STATE), ctx.dtype)
        y_c, hf_c, hb_c = bidir_ssd(xh_c, b_c, c_c, dtf_c, dtb_c, a_log[l], dt_bias[l], h0, h0, not last)

        h = x * (1 + sc1) + sh1
        proj = h @ w_in[l]
        xh, bm, cm, dtf, dtb = ssd_prepare(proj[..., :SCAN_COLS], conv_w[l], conv_b[l])
        y, _, _ = bidir_ssd(xh, bm, cm, dtf, dtb, a_log[l], dt_bias[l], hf_c, hb_c, True)
        mix = mixer_out(proj, y, xh, d_skip[l], ssd_norm_g[l], w_ssd_out[l], pool_w[l], pool_scale[l],
                        w_o[l], True)
        x = layer_norm(DEEPNORM_ALPHA * x + g1 * mix, ln_g[l, 0], ln_b[l, 0])

        h2 = x * (1 + sc2) + sh2
        x = layer_norm(DEEPNORM_ALPHA * x + g2 * peer(h2, w_q[l], sub_keys[l], u_tab[l], v_tab[l]),
                       ln_g[l, 1], ln_b[l, 1])

        if not last:
            mix_c = mixer_out(proj_c, y_c, xh_c, d_skip[l], ssd_norm_g[l], w_ssd_out[l], pool_w[l],
                              pool_scale[l], w_o[l], False)
            ctx = layer_norm(DEEPNORM_ALPHA * ctx + mods_c[2] * mix_c, ln_g[l, 0], ln_b[l, 0])
            h2c = ctx * (1 + mods_c[4]) + mods_c[3]
            ctx = layer_norm(DEEPNORM_ALPHA * ctx
                             + mods_c[5] * peer(h2c, w_q[l], sub_keys[l], u_tab[l], v_tab[l]),
                             ln_g[l, 1], ln_b[l, 1])
    return x


_drawn_inputs = setup_inputs


def setup_inputs(seed=0):
    import zlib

    import numpy as np

    out = dict(_drawn_inputs(seed))
    spreads = {}
    factors = {'ctx': 8.0,
     'c_ctx': 8.0,
     'b_mod': 4.752,
     'conv_b': 8.0,
     'd_skip': 90.797,
     'ssd_norm_g': 4.957,
     'pool_scale': 4.925}
    for name, (base, spread) in spreads.items():
        noise = np.random.default_rng([zlib.crc32(name.encode()), seed]).standard_normal(out[name].shape)
        drawn = base * np.exp(spread * noise) if base else spread * noise
        out[name] = __import__('jax').numpy.asarray(drawn.astype(out[name].dtype))
    for name, factor in factors.items():
        out[name] = (out[name] * factor).astype(out[name].dtype)
    return out
```

```python
from contextlib import ExitStack

import numpy as np

import concourse.bass as bass
from concourse import mybir

F32 = mybir.dt.float32
U32 = mybir.dt.uint32
ALU = mybir.AluOpType
ACT = mybir.ActivationFunctionType
AX_X = mybir.AxisListType.X

P = 128
D = 1024
KT = D // P
DEPTH = 2
SEQ, CTX_LEN, GRID_W = 512, 256, 64
ALPHA = (2.0 * DEPTH) ** 0.25
EPS = 1e-6
HEADS, HEAD_DIM, GROUPS = 16, 64, 4
HPG = HEADS // GROUPS
GW = HPG * HEAD_DIM
CONV_W = 5
SCAN_TILES = 16
X_TILES, B_TILES = 8, 4
POOL_WINDOWS = (2, 4, 8, 16)
PEER_HEADS, N_KEYS, TOPK = 8, 128, 16
N_EXPERTS = N_KEYS * N_KEYS
COL_DT, COL_Z = 2048, 2080
COL_POOL = COL_Z + D
WIDE = 512
PC_CONV, PC_BIAS, PC_SCALE, PC_NORM, PC_N = 0, 80, 96, 104, 112
HR_ALOG, HR_BIAS, HR_SKIP, HR_N = 0, 32, 64, 80
W_SCAN, W_Z, W_POOL, W_GP, W_GS, W_SSD, W_O, W_Q, W_MOD = 0, 4, 6, 7, 9, 11, 13, 15, 19
N_WIDE = W_MOD + 12
WIDE_SLOTS = 2
RING = 8
GRP = 4
PAD = 8
NEG = -3.0e38


class Bag:
    pass


class Signal:

    def __init__(self, k, name):
        self.sem = k.ctx.enter_context(k.nc.semaphore(name))
        self.base = 0

    def at(self, n):
        return self.base + n

    def advance(self, n):
        self.base += n


def setup(nc, ctx, io):
    k = Bag()
    k.nc, k.ctx, k.io, k.wide_plan, k.wide_next = nc, ctx, io, [], 0
    sb = lambda name, shape, dt=F32: ctx.enter_context(nc.sbuf_tensor(name, shape, dt))
    k.res = sb("residual", [P, 6, D])
    k.wide = sb("wide_blocks", [P, WIDE_SLOTS, KT, WIDE])
    k.ident = sb("identity", [P, P])
    k.tri = sb("triangles", [P, 2, P])
    k.ones = sb("ones", [P, P])
    k.zeros = sb("zeros", [P, WIDE])
    k.iota = sb("iota16", [P, TOPK])
    k.eps = sb("eps", [P, 1])
    k.hfin = sb("final_states", [P, 2, D])
    k.arena = sb("arena", [P, (207 - 24 - 32 - 14) * 256])
    k.ps = ctx.enter_context(nc.psum_tensor("banks", [P, 8, WIDE], F32))
    k.loaded = Signal(k, "loaded")
    k.mod_ready = Signal(k, "mod_ready")
    k.mod_used = Signal(k, "mod_used")
    k.mods_stored = Signal(k, "mods_stored")
    k.wide_used = Signal(k, "wide_used")
    k.xt_ready = Signal(k, "xt_ready")
    k.h_ready = Signal(k, "h_ready")
    k.proj_ready = Signal(k, "proj_ready")
    k.padded = Signal(k, "padded")
    k.conv_ready = Signal(k, "conv_ready")
    k.silu_done = Signal(k, "silu_done")
    k.turned = Signal(k, "turned")
    k.turn_copied = Signal(k, "turn_copied")
    k.dt_proj = Signal(k, "dt_proj")
    k.dt_copied = Signal(k, "dt_copied")
    k.z_proj = Signal(k, "z_proj")
    k.z_done = Signal(k, "z_done")
    k.consts_set = Signal(k, "consts_set")
    k.dt_vec = Signal(k, "dt_vec")
    k.dt_act = Signal(k, "dt_act")
    k.cum_ready = Signal(k, "cum_ready")
    k.xs_ready = Signal(k, "xs_ready")
    k.state_ready = Signal(k, "state_ready")
    k.state_added = Signal(k, "state_added")
    k.cb_ready = Signal(k, "cb_ready")
    k.cb_masked = Signal(k, "cb_masked")
    k.dtab_ready = Signal(k, "dtab_ready")
    k.acum_ready = Signal(k, "acum_ready")
    k.seg_ready = Signal(k, "seg_ready")
    k.m_ready = Signal(k, "m_ready")
    k.group_summed = Signal(k, "group_summed")
    k.y_ready = Signal(k, "y_ready")
    k.y_read = Signal(k, "y_read")
    k.inter_ready = Signal(k, "inter_ready")
    k.inter_read = Signal(k, "inter_read")
    k.gated = Signal(k, "gated")
    k.xd_ready = Signal(k, "xd_ready")
    k.rms_ready = Signal(k, "rms_ready")
    k.yn_ready = Signal(k, "yn_ready")
    k.yt_turned = Signal(k, "yt_turned")
    k.yt_copied = Signal(k, "yt_copied")
    k.pin_proj = Signal(k, "pin_proj")
    k.pin_copied = Signal(k, "pin_copied")
    k.mixed_ready = Signal(k, "mixed_ready")
    k.gp_proj = Signal(k, "gp_proj")
    k.gp_sig = Signal(k, "gp_sig")
    k.yp_proj = Signal(k, "yp_proj")
    k.merged0 = Signal(k, "merged0")
    k.gs_proj = Signal(k, "gs_proj")
    k.gs_sig = Signal(k, "gs_sig")
    k.ys_proj = Signal(k, "ys_proj")
    k.merged1 = Signal(k, "merged1")
    k.mix_proj = Signal(k, "mix_proj")
    k.mix_read = Signal(k, "mix_read")
    k.var_ready = Signal(k, "var_ready")
    k.std_ready = Signal(k, "std_ready")
    k.h2_ready = Signal(k, "h2_ready")
    k.h2_turned = Signal(k, "h2_turned")
    k.h2_copied = Signal(k, "h2_copied")
    k.q_proj = Signal(k, "q_proj")
    k.q_copied = Signal(k, "q_copied")
    k.s_proj = Signal(k, "s_proj")
    k.s_copied = Signal(k, "s_copied")
    k.idx_ready = Signal(k, "idx_ready")
    k.dots = Signal(k, "dots")
    k.gelus = Signal(k, "gelus")
    k.weights = Signal(k, "weights")
    k.diags = Signal(k, "diags")
    k.slot_free = Signal(k, "slot_free")
    k.acc_ready = Signal(k, "acc_ready")
    k.acc_read = Signal(k, "acc_read")
    k.top_ready = Signal(k, "top_ready")
    k.soft_done = Signal(k, "soft_done")
    k.pool_steps = Signal(k, "pool_steps")
    k.stored = Signal(k, "stored")
    k.decay_ready = Signal(k, "decay_ready")
    k.wide_landed = [Signal(k, f"wide_landed{i}") for i in range(WIDE_SLOTS)]
    k.landed = [Signal(k, f"row_landed{i}") for i in range(RING)]
    return k


def carve(k, *sizes):
    out, at = [], 0
    for words in sizes:
        out.append(k.arena[:, at:at + words])
        at += words
    assert at <= k.arena.shape[1], (at, k.arena.shape)
    return out


def bc(ap, shape):
    return ap.unsqueeze(2).to_broadcast(shape)


def load_wides(k, sp, upto):
    upto = min(upto, len(k.wide_plan))
    while k.wide_next < upto:
        n = k.wide_next
        layer, block = k.wide_plan[n]
        if n >= WIDE_SLOTS:
            sp.wait_ge(k.wide_used.sem, n - WIDE_SLOTS + 1)
        sp.dma_start(k.wide[:, n % WIDE_SLOTS].rearrange("p t c -> p (t c)"),
                     k.io["wide"][layer, block]).then_inc(k.wide_landed[n % WIDE_SLOTS].sem, 16)
        k.wide_next += 1


def take_wide(k, pe, n):
    pe.wait_ge(k.wide_landed[n % WIDE_SLOTS].sem, 16 * (n // WIDE_SLOTS + 1))
    return k.wide[:, n % WIDE_SLOTS]


def product(nc, out, lhs, rhs):
    for kt in range(KT):
        last = nc.tensor.matmul(out, lhs(kt), rhs(kt), start=(kt == 0), stop=(kt == KT - 1))
    return last


def stage_mods(k):
    nc, io = k.nc, k.io
    cvec, csil, brow = carve(k, KT * 2, KT * 2, DEPTH * 6 * D)
    cvec = cvec.rearrange("p (t s) -> p t s", s=2)
    csil = csil.rearrange("p (t s) -> p t s", s=2)
    brow = brow.rearrange("p (l c) -> p l c", l=DEPTH)
    n_blk = DEPTH * 12

    with nc.Block() as block:
        @block.sync
        def _(sp):
            for dst, src in ((cvec, io["cvec"]), (k.ident[:], io["ident"]), (k.tri[:], io["tri"]), (k.iota[:], io["iota"]),
                             (brow[0:1], io["b_mod"]), (brow[1:2], io["b_mod"])):
                sp.dma_start(dst, src).then_inc(k.loaded.sem, 16)
            load_wides(k, sp, 2)
            for t in range(6):
                sp.dma_start(k.res[:, t], io["tokens"][t]).then_inc(k.loaded.sem, 16)
            load_wides(k, sp, n_blk + WIDE_SLOTS)
            sp.wait_ge(k.mod_used.sem, n_blk)
            sp.dma_start(io["mods"].rearrange("l s c -> s l c"), brow[0:2]).then_inc(k.mods_stored.sem, 16)
            sp.wait_ge(k.mods_stored.sem, 16)
            sp.wait_ge(k.loaded.sem, 12 * 16)

        @block.scalar
        def _(act):
            act.wait_ge(k.loaded.sem, 12 * 16)
            nc.scalar.activation(csil, cvec, ACT.Silu).then_inc(k.h_ready.sem, 1)

        @block.gpsimd
        def _(pool):
            pool.memset(k.ones[:], 1.0)
            pool.memset(k.zeros[:], 0.0)
            pool.memset(k.eps[:], EPS).then_inc(k.consts_set.sem, 1)

        @block.tensor
        def _(pe):
            pe.wait_ge(k.h_ready.sem, 1)
            for n in range(n_blk):
                w = take_wide(k, pe, n)
                if n >= 2:
                    pe.wait_ge(k.mod_used.sem, n - 1)
                product(nc, k.ps[0:2, n % 2], lambda kt: csil[:, kt], lambda kt: w[:, kt]) \
                    .then_inc(k.mod_ready.sem, 1)
                pe.drain().then_inc(k.wide_used.sem, 1)

        @block.vector
        def _(dve):
            dve.wait_ge(k.loaded.sem, 12 * 16)
            for n in range(n_blk):
                row = brow[0:2, n // 12, (n % 12) * WIDE:(n % 12 + 1) * WIDE]
                dve.wait_ge(k.mod_ready.sem, n + 1)
                nc.vector.tensor_tensor(row, k.ps[0:2, n % 2], row, ALU.add).then_inc(k.mod_used.sem, 1)
    k.loaded.advance(12 * 16)
    k.h_ready.advance(1)
    k.consts_set.advance(1)
    return n_blk


def mixer_views(k):
    v = Bag()
    (hT, xtok, BT, CT, Btok, zs, hin, scr, pcols, hrow, wdt, modc, dts) = carve(
        k, 8 * 512, 4 * D, 4 * 512, 4 * 512, 4 * 512, 4 * D, 6 * D, 7680, PC_N, HR_N, KT * 32, 16, 4 * 288)
    r = lambda ap, n: ap.rearrange("p (a b) -> p a b", a=n)
    v.hT, v.xtok, v.BT, v.CT, v.Btok, v.zs = (r(hT, 8), r(xtok, 4), r(BT, 4), r(CT, 4), r(Btok, 4), r(zs, 4))
    v.hin = hin.rearrange("p (d c e) -> p d c e", d=2, c=3)
    v.pcols, v.hrow, v.wdt, v.modc = pcols, hrow, r(wdt, KT), r(modc, 2)
    v.scr = scr
    v.raw_xtok, v.raw_hin, v.raw_bc = xtok, hin, None
    v.dt, v.dta, v.e32, v.eac, v.dte, v.tmp32 = (r(dts[:, i * 128:(i + 1) * 128], 4) for i in range(6))
    v.cum = r(dts[:, 768:768 + 256], 4)
    v.ctot = r(dts[:, 1024:1024 + 128], 4)
    return v


def stage_project(k, layer, stream, w0, full):
    nc, io = k.nc, k.io
    T = SEQ if stream == 0 else CTX_LEN
    NT, tb = T // P, (2 if stream == 0 else 0)
    v = mixer_views(k)
    upad = v.scr[:, 0:2 * 520].rearrange("p (a b) -> p a b", a=2)
    acc = v.scr[:, 1040:1040 + 1024].rearrange("p (a b) -> p a b", a=2)
    sx = v.scr[:, 2064:2064 + 1024].rearrange("p (a b) -> p a b", a=2)
    mods = io["mods"][layer, stream]
    n_wide = 6 if full else 4
    ld = k.loaded.base
    zg = 2 * NT if full else 0

    def sx_or_bt(m):
        if m < X_TILES:
            return sx[:, m % 2, 0:T]
        if m < X_TILES + B_TILES:
            return v.BT[:, m - X_TILES, 0:T]
        return v.CT[:, m - X_TILES - B_TILES, 0:T]

    with nc.Block() as block:
        @block.sync
        def _(sp):
            sp.dma_start(v.modc, mods[0:2 * D].rearrange("(a t p) -> p a t", a=2, p=P),
                         allow_slow_non_contiguous=True).then_inc(k.loaded.sem, 16)
            sp.dma_start(v.pcols, io["pcols"][layer]).then_inc(k.loaded.sem, 16)
            sp.dma_start(v.hrow, io["hrows"][layer:layer + 1].to_broadcast([P, HR_N])).then_inc(k.loaded.sem, 16)
            sp.dma_start(v.wdt, io["w_dt"][layer]).then_inc(k.loaded.sem, 16)
            load_wides(k, sp, w0 + n_wide + WIDE_SLOTS)
            sp.wait_ge(k.loaded.sem, ld + 64)

        @block.tensor
        def _(pe):
            for kt in range(KT):
                if kt >= 2:
                    pe.wait_ge(k.h_ready.sem, k.h_ready.at(kt - 1))
                for t in range(NT):
                    last = nc.tensor.transpose(k.ps[:, kt % 2, t * P:(t + 1) * P],
                                               k.res[:, tb + t, kt * P:(kt + 1) * P], k.ident[:])
                last.then_inc(k.xt_ready.sem, 1)
            pe.wait_ge(k.h_ready.sem, k.h_ready.at(KT))
            pe.wait_ge(k.loaded.sem, ld + 64)

            def turn(m):
                src = sx_or_bt(m)
                pe.wait_ge(k.silu_done.sem, k.silu_done.at(m + 1))
                if m >= 2:
                    pe.wait_ge(k.turn_copied.sem, k.turn_copied.at(m - 1))
                for t in range(NT):
                    last = nc.tensor.transpose(k.ps[:, 4 + m % 2, t * P:(t + 1) * P],
                                               src[:, t * P:(t + 1) * P], k.ident[:])
                last.then_inc(k.turned.sem, 1)

            for m in range(SCAN_TILES):
                w = take_wide(k, pe, w0 + m // 4)
                if m >= 2:
                    pe.wait_ge(k.padded.sem, k.padded.at(m - 1))
                product(nc, k.ps[:, 2 + m % 2, 0:T], lambda kt: w[:, kt, (m % 4) * P:(m % 4 + 1) * P],
                        lambda kt: v.hT[:, kt, 0:T]).then_inc(k.proj_ready.sem, 1)
                if m % 4 == 3:
                    pe.drain().then_inc(k.wide_used.sem, 1)
                if 2 <= m < 2 + X_TILES + B_TILES:
                    turn(m - 2)
            for t in range(NT):
                last = product(nc, k.ps[:, 6, t * 32:(t + 1) * 32], lambda kt: v.hT[:, kt, t * P:(t + 1) * P],
                               lambda kt: v.wdt[:, kt])
            last.then_inc(k.dt_proj.sem, 1)
            pe.wait_ge(k.padded.sem, k.padded.at(SCAN_TILES))
            for n in range(zg):
                w = take_wide(k, pe, w0 + 4 + n // NT)
                if n >= 2:
                    pe.wait_ge(k.z_done.sem, k.z_done.at(n - 1))
                t = n % NT
                product(nc, k.ps[:, 2 + n % 2], lambda kt: v.hT[:, kt, t * P:(t + 1) * P],
                        lambda kt: w[:, kt]).then_inc(k.z_proj.sem, 1)
                if t == NT - 1:
                    pe.drain().then_inc(k.wide_used.sem, 1)

        @block.scalar
        def _(act):
            act.wait_ge(k.loaded.sem, ld + 64)
            act.wait_ge(k.consts_set.sem, k.consts_set.at(1))
            for kt in range(KT):
                act.wait_ge(k.xt_ready.sem, k.xt_ready.at(kt + 1))
                nc.scalar.activation(v.hT[:, kt, 0:T], k.ps[:, kt % 2, 0:T], ACT.Identity,
                                     bias=v.modc[:, 0, kt:kt + 1], scale=v.modc[:, 1, kt:kt + 1]) \
                    .then_inc(k.h_ready.sem, 1)
            for m in range(SCAN_TILES + 1):
                if m < SCAN_TILES:
                    act.wait_ge(k.proj_ready.sem, k.proj_ready.at(m + 1))
                    if m >= 2:
                        act.wait_ge(k.conv_ready.sem, k.conv_ready.at(m - 1))
                    nc.scalar.copy(upad[:, m % 2, 2:2 + T], k.ps[:, 2 + m % 2, 0:T]).then_inc(k.padded.sem, 1)
                if m >= 1:
                    act.wait_ge(k.conv_ready.sem, k.conv_ready.at(m))
                    if 2 < m <= X_TILES:
                        act.wait_ge(k.turned.sem, k.turned.at(m - 2))
                    nc.scalar.activation(sx_or_bt(m - 1), acc[:, (m - 1) % 2, 0:T], ACT.Silu,
                                         bias=v.pcols[:, PC_BIAS + m - 1:PC_BIAS + m]).then_inc(k.silu_done.sem, 1)
            act.wait_ge(k.dt_proj.sem, k.dt_proj.at(1))
            nc.scalar.copy(v.dt[:, 0:NT], k.ps[:, 6, 0:NT * 32].rearrange("p (t c) -> p t c", c=32)) \
                .then_inc(k.dt_copied.sem, 1)
            for n in range(zg):
                act.wait_ge(k.z_proj.sem, k.z_proj.at(n + 1))
                nc.scalar.activation(v.zs[:, n % NT, (n // NT) * WIDE:(n // NT + 1) * WIDE],
                                     k.ps[:, 2 + n % 2], ACT.Silu).then_inc(k.z_done.sem, 1)

        @block.vector
        def _(dve):
            nc.vector.memset(upad, 0.0)
            dve.wait_ge(k.loaded.sem, ld + 64)
            nc.vector.tensor_scalar(v.modc[:, 1], v.modc[:, 1], 1.0, None, ALU.add).then_inc(k.consts_set.sem, 1)

            def copy_turned(m):
                dve.wait_ge(k.turned.sem, k.turned.at(m + 1))
                dst = (v.xtok[:, 0:NT, m * P:(m + 1) * P] if m < X_TILES
                       else v.Btok[:, 0:NT, (m - X_TILES) * P:(m - X_TILES + 1) * P])
                nc.vector.tensor_copy(dst, k.ps[:, 4 + m % 2, 0:T].rearrange("p (t c) -> p t c", c=P)) \
                    .then_inc(k.turn_copied.sem, 1)

            for m in range(SCAN_TILES):
                dve.wait_ge(k.padded.sem, k.padded.at(m + 1))
                if m >= 2:
                    dve.wait_ge(k.silu_done.sem, k.silu_done.at(m - 1))
                a = acc[:, m % 2, 0:T]
                for j in range(CONV_W):
                    tap = v.pcols[:, PC_CONV + m * CONV_W + j:PC_CONV + m * CONV_W + j + 1]
                    u = upad[:, m % 2, j:j + T]
                    if j == 0:
                        last = nc.vector.tensor_scalar(a, u, tap, None, ALU.mult)
                    else:
                        dve.drain()
                        last = nc.vector.scalar_tensor_tensor(a, u, tap, a, ALU.mult, ALU.add)
                last.then_inc(k.conv_ready.sem, 1)
                if 2 <= m < 2 + X_TILES + B_TILES:
                    copy_turned(m - 2)
    k.loaded.advance(64)
    k.consts_set.advance(1)
    for s in (k.xt_ready, k.h_ready):
        s.advance(KT)
    for s in (k.proj_ready, k.padded, k.conv_ready, k.silu_done):
        s.advance(SCAN_TILES)
    for s in (k.turned, k.turn_copied):
        s.advance(X_TILES + B_TILES)
    for s in (k.dt_proj, k.dt_copied):
        s.advance(1)
    for s in (k.z_proj, k.z_done):
        s.advance(zg)
    return w0 + n_wide


def stage_states(k, stream):
    nc = k.nc
    T = SEQ if stream == 0 else CTX_LEN
    NT = T // P
    v = mixer_views(k)
    xs = v.scr[:, 0:2 * D].rearrange("p (a b) -> p a b", a=2)
    hsum = v.scr[:, 2 * D:3 * D]
    ctx = stream == 1
    steps = [(d, t, o) for d in range(2)
             for o, t in enumerate(range(NT) if d == 0 else reversed(range(NT)))
             if ctx or o < NT - 1]

    with nc.Block() as block:
        @block.vector
        def _(dve):
            dt, nt = v.dt[:, 0:NT], slice(0, NT)
            bias = v.hrow[:, HR_BIAS:HR_BIAS + 32].unsqueeze(1).to_broadcast([P, NT, 32])
            nc.vector.tensor_tensor(dt, dt, bias, ALU.add)
            dve.drain()
            nc.vector.scalar_tensor_tensor(v.e32[:, nt], dt, -1.0, dt, ALU.mult, ALU.min).then_inc(k.dt_vec.sem, 1)
            dve.wait_ge(k.dt_act.sem, k.dt_act.at(1))
            nc.vector.scalar_tensor_tensor(dt, dt, 0.0, v.tmp32[:, nt], ALU.max, ALU.add)
            dve.drain()
            ea = v.hrow[:, HR_ALOG:HR_ALOG + 32].unsqueeze(1).to_broadcast([P, NT, 32])
            nc.vector.scalar_tensor_tensor(v.dta[:, nt], dt, -1.0, ea, ALU.mult, ALU.mult).then_inc(k.dt_vec.sem, 1)
            dve.wait_ge(k.cum_ready.sem, k.cum_ready.at(1))
            nc.vector.tensor_copy(v.cum[:, nt], k.ps[:, 0, 0:NT * 64].rearrange("p (t c) -> p t c", c=64))
            dve.drain()
            nc.vector.tensor_tensor(v.e32[:, nt], v.cum[:, nt, 32:64], v.cum[:, nt, 0:32], ALU.subtract) \
                .then_inc(k.dt_vec.sem, 1)
            dve.wait_ge(k.dt_act.sem, k.dt_act.at(2))
            nc.vector.tensor_tensor(v.dte[:, nt], v.tmp32[:, nt], dt, ALU.mult)
            dve.drain()
            heads = lambda ap: ap.rearrange("p (h e) -> p h e", h=HEADS)

            def scale_x(n):
                d, t, _ = steps[n]
                if n >= 2:
                    dve.wait_ge(k.state_ready.sem, k.state_ready.at(n - 1))
                nc.vector.tensor_tensor(heads(xs[:, n % 2]), heads(v.xtok[:, t]),
                                        bc(v.dte[:, t, d * 16:d * 16 + 16], [P, HEADS, HEAD_DIM]), ALU.mult) \
                    .then_inc(k.xs_ready.sem, 1)

            scale_x(0)
            for n, (d, t, o) in enumerate(steps):
                if n + 1 < len(steps):
                    scale_x(n + 1)
                final = o == NT - 1
                dst = k.hfin[:, d] if final else v.hin[:, d, o]
                src = (k.hfin[:, d] if not ctx else None) if o == 0 else v.hin[:, d, o - 1]
                if src is not None:
                    nc.vector.tensor_tensor(heads(hsum), heads(src),
                                            bc(v.ctot[:, t, d * 16:d * 16 + 16], [P, HEADS, HEAD_DIM]), ALU.mult)
                    dve.drain()
                dve.wait_ge(k.state_ready.sem, k.state_ready.at(n + 1))
                st = k.ps[:, 2 + 2 * (n % 2):4 + 2 * (n % 2)].rearrange("p a b -> p (a b)")
                if src is not None:
                    last = nc.vector.tensor_tensor(dst, hsum, st, ALU.add)
                else:
                    last = nc.vector.tensor_copy(dst, st)
                last.then_inc(k.state_added.sem, 1)
                dve.drain()

        @block.scalar
        def _(act):
            nt = slice(0, NT)
            act.wait_ge(k.dt_vec.sem, k.dt_vec.at(1))
            nc.scalar.activation(v.e32[:, nt], v.e32[:, nt], ACT.Exp)
            nc.scalar.activation(v.hrow[:, HR_ALOG:HR_ALOG + 32], v.hrow[:, HR_ALOG:HR_ALOG + 32], ACT.Exp)
            act.drain()
            nc.scalar.activation(v.tmp32[:, nt], v.e32[:, nt], ACT.Ln, bias=k.ones[:, 0:1]).then_inc(k.dt_act.sem, 1)
            act.wait_ge(k.dt_vec.sem, k.dt_vec.at(3))
            nc.scalar.activation(v.tmp32[:, nt], v.e32[:, nt], ACT.Exp)
            nc.scalar.activation(v.eac[:, nt], v.cum[:, nt, 0:32], ACT.Exp)
            nc.scalar.activation(v.ctot[:, nt], v.cum[:, nt, 32:64], ACT.Exp).then_inc(k.dt_act.sem, 1)

        @block.tensor
        def _(pe):
            pe.wait_ge(k.dt_vec.sem, k.dt_vec.at(2))
            for t in range(NT):
                for d in range(2):
                    nc.tensor.matmul(k.ps[:, 0, t * 64 + d * 16:t * 64 + d * 16 + 16], k.tri[:, d],
                                     v.dta[:, t, d * 16:d * 16 + 16], start=True, stop=True)
                last = nc.tensor.matmul(k.ps[:, 0, t * 64 + 32:t * 64 + 64], k.ones[:], v.dta[:, t],
                                        start=True, stop=True)
            last.then_inc(k.cum_ready.sem, 1)
            for n, (d, t, o) in enumerate(steps):
                pe.wait_ge(k.xs_ready.sem, k.xs_ready.at(n + 1))
                if n >= 2:
                    pe.wait_ge(k.state_added.sem, k.state_added.at(n - 1))
                for g in range(GROUPS):
                    last = nc.tensor.matmul(k.ps[:, 2 + 2 * (n % 2) + g // 2, (g % 2) * GW:(g % 2 + 1) * GW],
                                            v.Btok[:, t, g * P:(g + 1) * P], xs[:, n % 2, g * GW:(g + 1) * GW],
                                            start=True, stop=True)
                last.then_inc(k.state_ready.sem, 1)
    k.dt_vec.advance(3)
    k.dt_act.advance(2)
    k.cum_ready.advance(1)
    for s in (k.xs_ready, k.state_ready, k.state_added):
        s.advance(len(steps))


def stage_outputs(k, stream):
    nc = k.nc
    T = SEQ if stream == 0 else CTX_LEN
    NT = T // P
    ctx = stream == 1
    v = mixer_views(k)
    s = v.scr
    cbm = s[:, 0:1024].rearrange("p (d c) -> p d c", d=2)
    dtab = s[:, 1024:2048].rearrange("p (a h c) -> p a h c", a=2, h=HPG)
    m_buf = s[:, 2048:3072].rearrange("p (a h c) -> p a h c", a=2, h=HPG)
    xd = s[:, 3072:3072 + 2 * D].rearrange("p (d c) -> p d c", d=2)
    ysum = s[:, 5120:5120 + D]
    ytmp = s[:, 6144:6144 + D]
    sq = s[:, 7168:7168 + 256]
    ss = v.e32[:, :, 0:GROUPS]
    heads = lambda ap: ap.rearrange("p (h e) -> p h e", h=HEADS)
    units = [(t, d, g) for t in range(NT) for d in range(2) for g in range(GROUPS)]
    order = lambda d, t: t if d == 0 else NT - 1 - t
    inters = [(t, d) for t in range(NT) for d in range(2) if not (ctx and order(d, t) == 0)]
    per = 2 * GROUPS
    Y, INT, CB = 2, 4, 6

    with nc.Block() as block:
        @block.gpsimd
        def _(pool):
            for n, (t, d, g) in enumerate(units):
                if n >= 2:
                    pool.wait_ge(k.acum_ready.sem, k.acum_ready.at(n - 1))
                h0 = d * 16 + g * HPG
                pool.tensor_copy(dtab[:, n % 2], bc(v.dta[:, t, h0:h0 + HPG], [P, HPG, P])) \
                    .then_inc(k.dtab_ready.sem, 1)
                if g == 0 and d == 0:
                    if t >= 1:
                        pool.wait_ge(k.y_ready.sem, k.y_ready.at(t))
                    for dd in range(2):
                        pool.tensor_tensor(heads(xd[:, dd]), heads(v.xtok[:, t]),
                                           bc(v.dt[:, t, dd * 16:dd * 16 + 16], [P, HEADS, HEAD_DIM]), ALU.mult) \
                            .then_inc(k.xd_ready.sem, 1)

        @block.tensor
        def _(pe):
            def intra(n):
                t, d, g = units[n]
                pe.wait_ge(k.m_ready.sem, k.m_ready.at(n + 1))
                pe.wait_ge(k.xd_ready.sem, k.xd_ready.at(2 * t + 2))
                if d == 0 and g == 0 and t >= 1:
                    pe.wait_ge(k.y_read.sem, k.y_read.at(t))
                for h in range(HPG):
                    hh = g * HPG + h
                    last = nc.tensor.matmul(k.ps[:, Y + g // 2, (hh % 8) * HEAD_DIM:(hh % 8 + 1) * HEAD_DIM],
                                            m_buf[:, n % 2, h], xd[:, d, hh * HEAD_DIM:(hh + 1) * HEAD_DIM],
                                            start=(d == 0 and hh % 8 == 0), stop=(d == 1 and hh % 8 == 7),
                                            skip_group_check=True)
                last.then_inc(k.y_ready.sem if g == GROUPS - 1 and d == 1 else k.group_summed.sem, 1)

            for n, (t, d, g) in enumerate(units):
                if d == 0 and g == 0:
                    if t >= 1:
                        pe.wait_ge(k.cb_masked.sem, k.cb_masked.at(t))
                    for gg in range(GROUPS):
                        last = nc.tensor.matmul(k.ps[:, CB, gg * P:(gg + 1) * P], v.BT[:, gg, t * P:(t + 1) * P],
                                                v.CT[:, gg, t * P:(t + 1) * P], start=True, stop=True)
                    last.then_inc(k.cb_ready.sem, 1)
                pe.wait_ge(k.dtab_ready.sem, k.dtab_ready.at(n + 1))
                if n >= 2:
                    pe.wait_ge(k.seg_ready.sem, k.seg_ready.at(n - 1))
                for h in range(HPG):
                    last = nc.tensor.matmul(k.ps[:, n % 2, h * P:(h + 1) * P], dtab[:, n % 2, h], k.tri[:, d],
                                            start=True, stop=True)
                last.then_inc(k.acum_ready.sem, 1)
                if n >= 1:
                    intra(n - 1)
                if g == 2 and (t, d) in inters:
                    i = inters.index((t, d))
                    if i >= 1:
                        pe.wait_ge(k.inter_read.sem, k.inter_read.at(i))
                    o = order(d, t)
                    h_in = k.hfin[:, d] if o == 0 else v.hin[:, d, o - 1]
                    for gg in range(GROUPS):
                        last = nc.tensor.matmul(k.ps[:, INT + gg // 2, (gg % 2) * GW:(gg % 2 + 1) * GW],
                                                v.CT[:, gg, t * P:(t + 1) * P], h_in[:, gg * GW:(gg + 1) * GW],
                                                start=True, stop=True)
                    last.then_inc(k.inter_ready.sem, 1)
            intra(len(units) - 1)

        @block.scalar
        def _(act):
            def squares(t):
                act.wait_ge(k.gated.sem, k.gated.at(t + 1))
                for g in range(GROUPS):
                    nc.scalar.activation(sq, v.zs[:, t, g * GW:(g + 1) * GW], ACT.Square,
                                         accum_out=ss[:, t, g:g + 1])
                    act.drain()

            for n, (t, d, g) in enumerate(units):
                act.wait_ge(k.acum_ready.sem, k.acum_ready.at(n + 1))
                if n >= 2:
                    tt, dd, gg = units[n - 2]
                    if (dd, gg) == (1, GROUPS - 1):
                        act.wait_ge(k.y_ready.sem, k.y_ready.at(tt + 1))
                    else:
                        act.wait_ge(k.group_summed.sem, k.group_summed.at(n - 1 - tt))
                for h in range(HPG):
                    col = d * 16 + g * HPG + h
                    last = nc.scalar.activation(m_buf[:, n % 2, h], k.ps[:, n % 2, h * P:(h + 1) * P], ACT.Relu,
                                                bias=v.cum[:, t, col:col + 1], scale=-1.0)
                last.then_inc(k.seg_ready.sem, 1)
                act.drain()
                nc.scalar.activation(m_buf[:, n % 2], m_buf[:, n % 2], ACT.Exp, scale=-1.0) \
                    .then_inc(k.decay_ready.sem, 1)
                if (d, g) == (0, 2) and t >= 1:
                    squares(t - 1)
            squares(NT - 1)

        @block.vector
        def _(dve):
            for n, (t, d, g) in enumerate(units):
                if d == 0 and g == 0:
                    dve.wait_ge(k.cb_ready.sem, k.cb_ready.at(t + 1))
                    cb = k.ps[:, CB].rearrange("p (g c) -> p g c", g=GROUPS)
                    for dd in range(2):
                        last = nc.vector.tensor_tensor(cbm[:, dd].rearrange("p (g c) -> p g c", g=GROUPS), cb,
                                                       k.tri[:, dd].unsqueeze(1).to_broadcast([P, GROUPS, P]),
                                                       ALU.mult)
                    last.then_inc(k.cb_masked.sem, 1)
                    dve.drain()
                dve.wait_ge(k.decay_ready.sem, k.decay_ready.at(n + 1))
                nc.vector.tensor_tensor(m_buf[:, n % 2], m_buf[:, n % 2],
                                        cbm[:, d, g * P:(g + 1) * P].unsqueeze(1).to_broadcast([P, HPG, P]),
                                        ALU.mult).then_inc(k.m_ready.sem, 1)
                if g == 0 and d == 0:
                    nc.vector.tensor_tensor(heads(ysum), heads(v.xtok[:, t]),
                                            bc(v.hrow[:, HR_SKIP:HR_SKIP + 16], [P, HEADS, HEAD_DIM]), ALU.mult)
                if g == 3 and (t, d) in inters:
                    i = inters.index((t, d))
                    dve.wait_ge(k.inter_ready.sem, k.inter_ready.at(i + 1))
                    nc.vector.tensor_tensor(heads(ytmp), heads(k.ps[:, INT:INT + 2].rearrange("p a b -> p (a b)")),
                                            bc(v.eac[:, t, d * 16:d * 16 + 16], [P, HEADS, HEAD_DIM]), ALU.mult) \
                        .then_inc(k.inter_read.sem, 1)
                    dve.drain()
                    nc.vector.tensor_tensor(ysum, ysum, ytmp, ALU.add)
                if g == 3 and d == 1:
                    dve.wait_ge(k.y_ready.sem, k.y_ready.at(t + 1))
                    dve.drain()
                    nc.vector.tensor_tensor(ysum, ysum, k.ps[:, Y:Y + 2].rearrange("p a b -> p (a b)"), ALU.add) \
                        .then_inc(k.y_read.sem, 1)
                    dve.drain()
                    nc.vector.tensor_tensor(v.zs[:, t], v.zs[:, t], ysum, ALU.mult).then_inc(k.gated.sem, 1)
    n = len(units)
    for x in (k.dtab_ready, k.acum_ready, k.seg_ready, k.decay_ready, k.m_ready):
        x.advance(n)
    for x in (k.y_ready, k.y_read, k.gated, k.cb_ready, k.cb_masked):
        x.advance(NT)
    k.group_summed.advance(n - NT)
    k.xd_ready.advance(2 * NT)
    for x in (k.inter_ready, k.inter_read):
        x.advance(len(inters))


def layer_norm(k, dve, row, stats, g_row, b_row, n):
    nc = k.nc
    dve.drain()
    nc.vector.bn_stats(stats[:, 0:6], row[:, 0:512])
    nc.vector.bn_stats(stats[:, 6:12], row[:, 512:1024])
    dve.drain()
    nc.vector.bn_aggr(stats[:, 12:14], stats[:, 0:12]).then_inc(k.var_ready.sem, 1)
    dve.wait_ge(k.std_ready.sem, k.std_ready.at(n + 1))
    nc.vector.reciprocal(stats[:, 15:16], stats[:, 14:15])
    dve.drain()
    nc.vector.tensor_scalar(row, row, stats[:, 12:13], stats[:, 15:16], ALU.subtract, ALU.mult)
    dve.drain()
    nc.vector.tensor_tensor(row, row, g_row, ALU.mult)
    dve.drain()
    nc.vector.tensor_tensor(row, row, b_row, ALU.add)


def norm_root(k, act, stats, n):
    act.wait_ge(k.var_ready.sem, k.var_ready.at(n + 1))
    k.nc.scalar.activation(stats[:, 14:15], stats[:, 13:14], ACT.Sqrt, bias=k.eps[:]).then_inc(k.std_ready.sem, 1)


def stage_merge(k, layer, stream, w0):
    nc, io = k.nc, k.io
    T = SEQ if stream == 0 else CTX_LEN
    NT, tb = T // P, (2 if stream == 0 else 0)
    grid = stream == 0
    ROWS, COLS = (SEQ // GRID_W, GRID_W) if grid else (1, CTX_LEN)
    v = mixer_views(k)
    s = v.scr
    ld = k.loaded.base
    pool_w = s[:, 0:1024].rearrange("p (g c) -> p g c", g=4)
    icnt = s[:, 1024:1024 + 2048].rearrange("p (g c) -> p g c", g=4)[:, :, 0:T]
    sig = s[:, 3072:3072 + 1024].rearrange("p (a b) -> p a b", a=2)
    g1row, lng, lnb = (s[:, 4096 + i * D:4096 + (i + 1) * D] for i in range(3))
    stats = s[:, 7168:7168 + 16]
    rms = s[:, 7200:7216].rearrange("p (t g) -> p t g", g=4)
    rinv = s[:, 7216:7232].rearrange("p (t g) -> p t g", g=4)
    SW = COLS + 2 * PAD
    pa = k.arena[:, 8192:8192 + ROWS * SW].rearrange("p (r c) -> p r c", r=ROWS)
    pb = k.arena[:, 8192 + 640:8192 + 640 + ROWS * SW].rearrange("p (r c) -> p r c", r=ROWS)
    pin = k.arena[:, 8192 + 1280:8192 + 1280 + T]
    ra = k.arena[:, 10240:10240 + 1536].rearrange("p (r c) -> p r c", r=24)
    rb = k.arena[:, 12288:12288 + 1536].rearrange("p (r c) -> p r c", r=24)
    tmp = k.arena[:, 12288 + 1536:12288 + 2048]
    sgs = v.xtok.rearrange("p a b -> p (a b)").rearrange("p (m c) -> p m c", m=8)
    hin = v.raw_hin
    yT = v.zs.rearrange("p a b -> p (a b)")
    merged = hin[:, 0:4096].rearrange("p (m c) -> p m c", m=8)
    mixed = hin[:, 4096:6144].rearrange("p (g c) -> p g c", g=4)
    yT = v.hT
    mods = io["mods"][layer, stream]

    with nc.Block() as block:
        @block.sync
        def _(sp):
            sp.dma_start(pool_w, io["pool_w"][layer]).then_inc(k.loaded.sem, 16)
            ic = (io["icnt_grid"] if grid else io["icnt_line"])
            sp.dma_start(icnt, ic.unsqueeze(0).to_broadcast([P, 4, T])).then_inc(k.loaded.sem, 16)
            for dst, src in ((g1row, mods[2 * D:3 * D]), (lng, io["ln_g"][layer, 0]), (lnb, io["ln_b"][layer, 0])):
                sp.dma_start(dst, src.unsqueeze(0).to_broadcast([P, D])).then_inc(k.loaded.sem, 16)
            load_wides(k, sp, w0 + 9 + WIDE_SLOTS)
            sp.wait_ge(k.loaded.sem, ld + 80)

        @block.tensor
        def _(pe):
            w = take_wide(k, pe, w0)
            for g in range(4):
                if g >= 2:
                    pe.wait_ge(k.pin_copied.sem, k.pin_copied.at(g - 1))
                product(nc, k.ps[:, g % 2, 0:T], lambda kt: w[:, kt, g * P:(g + 1) * P],
                        lambda kt: v.hT[:, kt, 0:T]).then_inc(k.pin_proj.sem, 1)
            pe.drain().then_inc(k.wide_used.sem, 1)
            pe.wait_ge(k.loaded.sem, ld + 80)
            for m in range(8):
                w = take_wide(k, pe, w0 + 1 + m // 4)
                if m >= 2:
                    pe.wait_ge(k.merged0.sem, k.merged0.at(m - 1))
                product(nc, k.ps[:, 2 + m % 2, 0:T], lambda kt: w[:, kt, (m % 4) * P:(m % 4 + 1) * P],
                        lambda kt: v.hT[:, kt, 0:T]).then_inc(k.gp_proj.sem, 1)
                if m % 4 == 3:
                    pe.drain().then_inc(k.wide_used.sem, 1)
                pe.wait_ge(k.mixed_ready.sem, k.mixed_ready.at(m // 2 + 1))
                nc.tensor.matmul(k.ps[:, 4 + m % 2, 0:T], pool_w[:, m // 2, (m % 2) * P:(m % 2 + 1) * P],
                                 mixed[:, m // 2, 0:T], start=True, stop=True).then_inc(k.yp_proj.sem, 1)
            pe.wait_ge(k.pin_copied.sem, k.pin_copied.at(4))
            for m in range(8):
                w = take_wide(k, pe, w0 + 3 + m // 4)
                if m >= 2:
                    pe.wait_ge(k.gs_sig.sem, k.gs_sig.at(m - 1))
                product(nc, k.ps[:, m % 2, 0:T], lambda kt: w[:, kt, (m % 4) * P:(m % 4 + 1) * P],
                        lambda kt: v.hT[:, kt, 0:T]).then_inc(k.gs_proj.sem, 1)
                if m % 4 == 3:
                    pe.drain().then_inc(k.wide_used.sem, 1)
            for kt in range(KT):
                pe.wait_ge(k.yn_ready.sem, k.yn_ready.at(NT))
                if kt >= 2:
                    pe.wait_ge(k.yt_copied.sem, k.yt_copied.at(kt - 1))
                for t in range(NT):
                    last = nc.tensor.transpose(k.ps[:, 6 + kt % 2, t * P:(t + 1) * P],
                                               v.zs[:, t, kt * P:(kt + 1) * P], k.ident[:])
                last.then_inc(k.yt_turned.sem, 1)
            pe.wait_ge(k.yt_copied.sem, k.yt_copied.at(KT))
            pe.wait_ge(k.merged0.sem, k.merged0.at(8))
            for m in range(8):
                w = take_wide(k, pe, w0 + 5 + m // 4)
                if m >= 2:
                    pe.wait_ge(k.merged1.sem, k.merged1.at(m - 1))
                product(nc, k.ps[:, 2 + m % 2, 0:T], lambda kt: w[:, kt, (m % 4) * P:(m % 4 + 1) * P],
                        lambda kt: yT[:, kt, 0:T]).then_inc(k.ys_proj.sem, 1)
                if m % 4 == 3:
                    pe.drain().then_inc(k.wide_used.sem, 1)
            pe.wait_ge(k.merged1.sem, k.merged1.at(8))
            pe.wait_ge(k.gs_sig.sem, k.gs_sig.at(8))
            for n in range(2 * NT):
                w = take_wide(k, pe, w0 + 7 + n // NT)
                if n >= 2:
                    pe.wait_ge(k.mix_read.sem, k.mix_read.at(n - 1))
                t = n % NT
                product(nc, k.ps[:, n % 2], lambda kt: merged[:, kt, t * P:(t + 1) * P],
                        lambda kt: w[:, kt]).then_inc(k.mix_proj.sem, 1)
                if t == NT - 1:
                    pe.drain().then_inc(k.wide_used.sem, 1)

        @block.scalar
        def _(act):
            nc.scalar.activation(rms[:, 0:NT], v.e32[:, 0:NT, 0:GROUPS], ACT.Sqrt, bias=k.eps[:],
                                 scale=1.0 / GW).then_inc(k.rms_ready.sem, 1)
            for g in range(4):
                act.wait_ge(k.pin_proj.sem, k.pin_proj.at(g + 1))
                if g >= 1:
                    act.wait_ge(k.mixed_ready.sem, k.mixed_ready.at(g))
                else:
                    act.wait_ge(k.consts_set.sem, k.consts_set.at(1))
                nc.scalar.copy(pa[:, :, PAD:PAD + COLS], k.ps[:, g % 2, 0:T].rearrange("p (r c) -> p r c", r=ROWS))
                nc.scalar.copy(pin, k.ps[:, g % 2, 0:T]).then_inc(k.pin_copied.sem, 1)
            for m in range(8):
                act.wait_ge(k.gp_proj.sem, k.gp_proj.at(m + 1))
                if m >= 2:
                    act.wait_ge(k.merged0.sem, k.merged0.at(m - 1))
                nc.scalar.activation(sig[:, m % 2, 0:T], k.ps[:, 2 + m % 2, 0:T], ACT.Sigmoid) \
                    .then_inc(k.gp_sig.sem, 1)
            for m in range(8):
                act.wait_ge(k.gs_proj.sem, k.gs_proj.at(m + 1))
                nc.scalar.activation(sgs[:, m, 0:T], k.ps[:, m % 2, 0:T], ACT.Sigmoid).then_inc(k.gs_sig.sem, 1)
            for kt in range(KT):
                act.wait_ge(k.yt_turned.sem, k.yt_turned.at(kt + 1))
                nc.scalar.activation(yT[:, kt, 0:T], k.ps[:, 6 + kt % 2, 0:T], ACT.Copy,
                                     scale=v.pcols[:, PC_NORM + kt:PC_NORM + kt + 1]).then_inc(k.yt_copied.sem, 1)
            for t in range(NT):
                norm_root(k, act, stats, t)

        @block.vector
        def _(dve):
            nc.vector.memset(pa, 0.0)
            nc.vector.memset(ra, 0.0)
            nc.vector.memset(rb, 0.0).then_inc(k.consts_set.sem, 1)
            dve.wait_ge(k.rms_ready.sem, k.rms_ready.at(1))
            nc.vector.reciprocal(rinv[:, 0:NT], rms[:, 0:NT])
            dve.drain()
            for t in range(NT):
                y = v.zs[:, t].rearrange("p (g c) -> p g c", g=GROUPS)
                nc.vector.tensor_tensor(y, y, bc(rinv[:, t], [P, GROUPS, GW]), ALU.mult).then_inc(k.yn_ready.sem, 1)
            dve.wait_ge(k.loaded.sem, ld + 80)
            for g, win in enumerate(POOL_WINDOWS):
                dve.wait_ge(k.pin_copied.sem, k.pin_copied.at(g + 1))
                src, dst, lo, hi, left, right = pa, pb, 1, SW, 1, 0
                w = 2
                while True:
                    n = hi - lo
                    nc.vector.tensor_tensor(dst[:, :, lo:hi], src[:, :, lo - left:lo - left + n],
                                            src[:, :, lo + right:lo + right + n], ALU.add)
                    dve.drain()
                    src, dst = dst, (pa if dst is pb else pb)
                    if w == win:
                        break
                    left = right = w // 2
                    lo, hi = lo + left, hi - right
                    w *= 2
                box = src[:, :, PAD:PAD + COLS]
                if grid:
                    nc.vector.tensor_copy(ra[:, PAD:PAD + ROWS], box)
                    dve.drain()
                    src, dst, lo, hi, left, right = ra, rb, 1, ROWS + 2 * PAD, 1, 0
                    w = 2
                    while True:
                        n = hi - lo
                        nc.vector.tensor_tensor(dst[:, lo:hi], src[:, lo - left:lo - left + n],
                                                src[:, lo + right:lo + right + n], ALU.add)
                        dve.drain()
                        src, dst = dst, src
                        if w == win:
                            break
                        left = right = w // 2
                        lo, hi = lo + left, hi - right
                        w *= 2
                    box = src[:, PAD:PAD + ROWS]
                rows = lambda ap: ap.rearrange("p (r c) -> p r c", r=ROWS)
                nc.vector.tensor_tensor(rows(tmp[:, 0:T]), box, rows(icnt[:, g]), ALU.mult)
                dve.drain()
                if grid and g < 3:
                    nc.vector.memset(ra, 0.0)
                    nc.vector.memset(rb, 0.0)
                nc.vector.memset(pa, 0.0)
                nc.vector.tensor_tensor(mixed[:, g, 0:T], tmp[:, 0:T], pin, ALU.subtract) \
                    .then_inc(k.mixed_ready.sem, 1)
            for m in range(8):
                dve.wait_ge(k.yp_proj.sem, k.yp_proj.at(m + 1))
                dve.wait_ge(k.gp_sig.sem, k.gp_sig.at(m + 1))
                nc.vector.scalar_tensor_tensor(merged[:, m, 0:T], k.ps[:, 4 + m % 2, 0:T],
                                               v.pcols[:, PC_SCALE + m:PC_SCALE + m + 1], sig[:, m % 2, 0:T],
                                               ALU.mult, ALU.mult).then_inc(k.merged0.sem, 1)
            dve.wait_ge(k.gs_sig.sem, k.gs_sig.at(8))
            for m in range(8):
                dve.wait_ge(k.ys_proj.sem, k.ys_proj.at(m + 1))
                dve.drain()
                nc.vector.tensor_tensor(tmp[:, 0:T], k.ps[:, 2 + m % 2, 0:T], sgs[:, m, 0:T], ALU.mult)
                dve.drain()
                nc.vector.tensor_tensor(merged[:, m, 0:T], merged[:, m, 0:T], tmp[:, 0:T], ALU.add) \
                    .then_inc(k.merged1.sem, 1)
            for n in range(2 * NT):
                t, half = n % NT, slice((n // NT) * WIDE, (n // NT + 1) * WIDE)
                dve.wait_ge(k.mix_proj.sem, k.mix_proj.at(n + 1))
                dve.drain()
                nc.vector.tensor_tensor(tmp, k.ps[:, n % 2], g1row[:, half], ALU.mult).then_inc(k.mix_read.sem, 1)
                dve.drain()
                x = k.res[:, tb + t, half]
                nc.vector.scalar_tensor_tensor(x, x, ALPHA, tmp, ALU.mult, ALU.add)
                if n >= NT:
                    layer_norm(k, dve, k.res[:, tb + t], stats, lng, lnb, t)
    k.loaded.advance(80)
    k.consts_set.advance(1)
    k.rms_ready.advance(1)
    for x in (k.pin_copied, k.mixed_ready, k.pin_proj):
        x.advance(4)
    for x in (k.gp_proj, k.gp_sig, k.yp_proj, k.merged0, k.gs_proj, k.gs_sig, k.ys_proj, k.merged1,
              k.yt_turned, k.yt_copied):
        x.advance(8)
    for x in (k.mix_proj, k.mix_read):
        x.advance(2 * NT)
    for x in (k.var_ready, k.std_ready, k.yn_ready):
        x.advance(NT)
    return w0 + 9


def peer_views(k, NT):
    v = Bag()
    ring, h2, scores, g2, lng, lnb, dg, small = carve(
        k, RING * 2 * D, 4 * D, 4 * 2048 + 256, D, D, D, 8 * P, 2000)
    v.ring = ring.rearrange("p (s c) -> p s c", s=RING)
    v.raw_ring = ring
    v.h2 = h2.rearrange("p (t c) -> p t c", t=4)
    v.scores, v.g2, v.lng, v.lnb = scores, g2, lng, lnb
    v.diag = dg.rearrange("p (s c) -> p s c", s=8)
    v.small = small
    return v


def stage_queries(k, layer, stream, w0):
    nc, io = k.nc, k.io
    T = SEQ if stream == 0 else CTX_LEN
    NT, tb = T // P, (2 if stream == 0 else 0)
    v = peer_views(k, NT)
    ld = k.loaded.base
    mods = io["mods"][layer, stream]
    h2T = v.raw_ring[:, 0:4096].rearrange("p (a b) -> p a b", a=8)
    keys = v.raw_ring[:, 4096:6144].rearrange("p (a b) -> p a b", a=16)
    qT = v.raw_ring[:, 6144:7168].rearrange("p (a b) -> p a b", a=2)
    sh2, sc2 = v.raw_ring[:, 7168:8192], v.raw_ring[:, 8192:9216]
    M = 2 * PEER_HEADS

    with nc.Block() as block:
        @block.sync
        def _(sp):
            for dst, src in ((sh2, mods[3 * D:4 * D]), (sc2, mods[4 * D:5 * D]), (v.g2, mods[5 * D:6 * D]),
                             (v.lng, io["ln_g"][layer, 1]), (v.lnb, io["ln_b"][layer, 1])):
                sp.dma_start(dst, src.unsqueeze(0).to_broadcast([P, D])).then_inc(k.loaded.sem, 16)
            sp.dma_start(keys, io["keys"][layer]).then_inc(k.loaded.sem, 16)
            load_wides(k, sp, w0 + 4 + WIDE_SLOTS)
            sp.wait_ge(k.loaded.sem, ld + 96)

        @block.vector
        def _(dve):
            nc.vector.memset(v.scores[:, NT * 2048:NT * 2048 + 256], 0.0)
            dve.wait_ge(k.loaded.sem, ld + 96)
            for t in range(NT):
                nc.vector.scalar_tensor_tensor(v.h2[:, t], sc2, 1.0, k.res[:, tb + t], ALU.add, ALU.mult)
                dve.drain()
                nc.vector.tensor_tensor(v.h2[:, t], v.h2[:, t], sh2, ALU.add).then_inc(k.h2_ready.sem, 1)
            for m in range(M):
                dve.wait_ge(k.s_proj.sem, k.s_proj.at(m + 1))
                dst = v.scores[:, 0:NT * 2048].rearrange("p (t c) -> p t c", t=NT)[:, :, m * P:(m + 1) * P]
                nc.vector.tensor_copy(dst, k.ps[:, 4 + m % 2, 0:T].rearrange("p (t c) -> p t c", c=P)) \
                    .then_inc(k.s_copied.sem, 1)

        @block.scalar
        def _(act):
            for kt in range(KT):
                act.wait_ge(k.h2_turned.sem, k.h2_turned.at(kt + 1))
                nc.scalar.copy(h2T[:, kt, 0:T], k.ps[:, kt % 2, 0:T]).then_inc(k.h2_copied.sem, 1)
            for m in range(M):
                act.wait_ge(k.q_proj.sem, k.q_proj.at(m + 1))
                if m >= 2:
                    act.wait_ge(k.s_proj.sem, k.s_proj.at(m - 1))
                nc.scalar.copy(qT[:, m % 2, 0:T], k.ps[:, 2 + m % 2, 0:T]).then_inc(k.q_copied.sem, 1)

        @block.tensor
        def _(pe):
            pe.wait_ge(k.h2_ready.sem, k.h2_ready.at(NT))
            for kt in range(KT):
                if kt >= 2:
                    pe.wait_ge(k.h2_copied.sem, k.h2_copied.at(kt - 1))
                for t in range(NT):
                    last = nc.tensor.transpose(k.ps[:, kt % 2, t * P:(t + 1) * P], v.h2[:, t, kt * P:(kt + 1) * P],
                                               k.ident[:])
                last.then_inc(k.h2_turned.sem, 1)
            pe.wait_ge(k.h2_copied.sem, k.h2_copied.at(KT))
            pe.wait_ge(k.loaded.sem, ld + 96)

            def score(m):
                pe.wait_ge(k.q_copied.sem, k.q_copied.at(m + 1))
                if m >= 2:
                    pe.wait_ge(k.s_copied.sem, k.s_copied.at(m - 1))
                for t in range(NT):
                    last = nc.tensor.matmul(k.ps[:, 4 + m % 2, t * P:(t + 1) * P], qT[:, m % 2, t * P:(t + 1) * P],
                                            keys[:, m], start=True, stop=True)
                last.then_inc(k.s_proj.sem, 1)

            for m in range(M):
                w = take_wide(k, pe, w0 + m // 4)
                if m >= 2:
                    pe.wait_ge(k.q_copied.sem, k.q_copied.at(m - 1))
                product(nc, k.ps[:, 2 + m % 2, 0:T], lambda kt: w[:, kt, (m % 4) * P:(m % 4 + 1) * P],
                        lambda kt: h2T[:, kt, 0:T]).then_inc(k.q_proj.sem, 1)
                if m % 4 == 3:
                    pe.drain().then_inc(k.wide_used.sem, 1)
                if m >= 1:
                    score(m - 1)
            score(M - 1)
    k.loaded.advance(96)
    k.h2_ready.advance(NT)
    for x in (k.h2_turned, k.h2_copied):
        x.advance(KT)
    for x in (k.q_proj, k.q_copied, k.s_proj, k.s_copied):
        x.advance(M)
    return w0 + 4


def stage_retrieve(k, layer, stream, last_stage):
    nc, io = k.nc, k.io
    T = SEQ if stream == 0 else CTX_LEN
    NT, tb = T // P, (2 if stream == 0 else 0)
    v = peer_views(k, NT)
    UNITS = NT * PEER_HEADS
    SEL = UNITS * TOPK
    ROUNDS = SEL // RING
    at = [0]

    def small(n, dt=F32):
        a = v.small[:, at[0]:at[0] + n]
        at[0] += n
        return a if dt == F32 else a.bitcast(dt)

    sc, sc2 = small(256), small(256)
    sv, si, sif = small(32), small(32, U32), small(32)
    cand, cand2 = small(256), small(256)
    tv, tp = small(16), small(16, U32)
    ab, abf, hot, pair = small(32, U32), small(32), small(512), small(32)
    nmax, esum, einv = small(1), small(1), small(1)
    idf = small(16)
    idx, gate = small(32, U32), small(32)
    act_in, gel, wgt = small(32), small(32), small(32)
    stats = small(16)

    def top16(dve, val, ind, src, spare):
        nc.vector.max(val[:, 0:8], src)
        dve.drain()
        nc.vector.max_index(ind[:, 0:8], val[:, 0:8], src)
        nc.vector.match_replace(spare, val[:, 0:8], src, NEG)
        dve.drain()
        nc.vector.max(val[:, 8:16], spare)
        dve.drain()
        nc.vector.max_index(ind[:, 8:16], val[:, 8:16], spare)

    def choose_a(dve, score_ap):
        nc.vector.tensor_copy(sc, score_ap)
        dve.drain()
        for half in range(2):
            top16(dve, sv[:, half * 16:half * 16 + 16], si[:, half * 16:half * 16 + 16],
                  sc[:, half * P:(half + 1) * P], sc2[:, half * P:(half + 1) * P])
        dve.drain()
        nc.vector.tensor_copy(sif, si)

    def choose_b(dve, par, unit):
        c3 = cand.rearrange("p (a b) -> p a b", a=TOPK)
        nc.vector.tensor_tensor(c3, bc(sv[:, 0:16], [P, TOPK, TOPK]),
                                sv[:, 16:32].unsqueeze(1).to_broadcast([P, TOPK, TOPK]), ALU.add)
        dve.drain()
        top16(dve, tv, tp, cand, cand2)
        nc.vector.tensor_scalar(nmax, tv[:, 0:1], -1.0, None, ALU.mult).then_inc(k.top_ready.sem, 1)
        dve.drain()
        nc.vector.tensor_scalar(ab[:, 0:16], tp, 4, None, ALU.logical_shift_right)
        nc.vector.tensor_scalar(ab[:, 16:32], tp, 15, None, ALU.bitwise_and)
        dve.drain()
        nc.vector.tensor_copy(abf, ab)
        dve.drain()
        h3 = hot.rearrange("p (s b) -> p s b", b=TOPK)
        nc.vector.tensor_tensor(h3, bc(abf, [P, 32, TOPK]), k.iota[:].unsqueeze(1).to_broadcast([P, 32, TOPK]),
                                ALU.is_equal)
        dve.drain()
        h4 = hot.rearrange("p (z s b) -> p z s b", z=2, b=TOPK)
        s4 = sif.rearrange("p (z b) -> p z b", z=2).unsqueeze(2).to_broadcast([P, 2, TOPK, TOPK])
        nc.vector.tensor_tensor(h4, h4, s4, ALU.mult)
        dve.drain()
        nc.vector.tensor_reduce(pair, h3, AX_X, ALU.add)
        dve.drain()
        nc.vector.scalar_tensor_tensor(idf, pair[:, 0:16], float(N_KEYS), pair[:, 16:32], ALU.mult, ALU.add)
        dve.drain()
        nc.vector.tensor_scalar(idx[:, par * 16:par * 16 + 16], idf, float(layer * N_EXPERTS), None, ALU.add) \
            .then_inc(k.idx_ready.sem, 1)
        dve.wait_ge(k.soft_done.sem, unit + 1)
        nc.vector.reciprocal(einv, esum)
        dve.drain()
        g = gate[:, par * 16:par * 16 + 16]
        nc.vector.tensor_scalar(g, g, einv, None, ALU.mult)

    def softmax(act, par, unit):
        act.wait_ge(k.top_ready.sem, unit + 1)
        nc.scalar.activation(gate[:, par * 16:par * 16 + 16], tv, ACT.Exp, bias=nmax,
                             accum_out=esum).then_inc(k.soft_done.sem, 1)

    s0 = k.slot_free.base
    u0, r0, d0, q0 = (k.idx_ready.base, k.landed[0].base // 16, k.diags.base, k.dots.base)

    with nc.Block() as block:
        @block.gpsimd
        def _(pool):
            for t in range(NT):
                with pool.Fori(0, PEER_HEADS // 2) as i:
                    for par in range(2):
                        pool.wait_ge(k.idx_ready.sem, i * 2 + (u0 + t * 8 + par + 1))
                        pool.sem_inc(k.pool_steps.sem, 1)
                        for j in range(TOPK):
                            pool.wait_ge(k.slot_free.sem, i * 32 + (s0 + t * 128 + par * 16 + j + 1))
                            pool.sem_inc(k.pool_steps.sem, 1)
                            pool.indirect_dma_start(
                                out=v.ring[:, j % RING], out_offset=None, in_=io["experts"],
                                in_offset=bass.IndirectOffsetOnAxis(
                                    ap=idx[:, par * 16 + j:par * 16 + j + 1], axis=0),
                            ).then_inc(k.landed[j % RING].sem, 16)

        @block.vector
        def _(dve):
            def finish(t):
                dve.wait_ge(k.acc_ready.sem, k.acc_ready.at(t + 1))
                x = k.res[:, tb + t]
                a = 2 * (t % 2)
                wsum = v.h2[:, t]
                nc.vector.tensor_tensor(wsum, k.ps[:, a:a + 2].rearrange("p a b -> p (a b)"), v.g2, ALU.mult) \
                    .then_inc(k.acc_read.sem, 1)
                dve.drain()
                nc.vector.scalar_tensor_tensor(x, x, ALPHA, wsum, ALU.mult, ALU.add)
                layer_norm(k, dve, x, stats, v.lng, v.lnb, t)
                dve.drain().then_inc(k.stored.sem, 1)

            choose_a(dve, v.scores[:, 0:256])
            dve.drain()
            choose_b(dve, 0, u0)
            for t in range(NT):
                with dve.Fori(0, PEER_HEADS // 2) as i:
                    for par in range(2):
                        for q in range(TOPK // GRP):
                            for j in range(q * GRP, (q + 1) * GRP):
                                slot = j % RING
                                dve.wait_ge(k.landed[slot].sem,
                                            i * 64 + 16 * (r0 + t * 16 + par * 2 + j // RING + 1))
                                u_row = v.ring[:, slot, 0:D]
                                last = nc.vector.tensor_tensor_reduce(
                                    out=u_row, in0=u_row, in1=v.h2[:, t], scale=1.0, scalar=0.0,
                                    op0=ALU.mult, op1=ALU.add, accum_out=act_in[:, j:j + 1])
                            last.then_inc(k.dots.sem, 1)
                            dve.wait_ge(k.gelus.sem, i * 8 + (q0 + t * 32 + par * 4 + q + 1))
                            nc.vector.tensor_tensor(wgt[:, j - 3:j + 1], gel[:, j - 3:j + 1],
                                                    gate[:, par * 16 + j - 3:par * 16 + j + 1], ALU.mult) \
                                .then_inc(k.weights.sem, 1)
                            if q == 0:
                                choose_a(dve, v.scores[:, bass.ds(i * 512 + (t * 2048 + (par + 1) * 256), 256)])
                            if q == 1:
                                choose_b(dve, 1 - par, i * 2 + (u0 + t * 8 + par + 1))
                            dve.drain()
                if t >= 1:
                    finish(t - 1)
            finish(NT - 1)

        @block.scalar
        def _(act):
            softmax(act, 0, u0)
            for t in range(NT):
                with act.Fori(0, PEER_HEADS // 2) as i:
                    for par in range(2):
                        for q in range(TOPK // GRP):
                            n = i * 8 + (q0 + t * 32 + par * 4 + q + 1)
                            act.wait_ge(k.dots.sem, n)
                            nc.scalar.activation(gel[:, q * GRP:(q + 1) * GRP], act_in[:, q * GRP:(q + 1) * GRP],
                                                 ACT.Gelu_apprx_tanh).then_inc(k.gelus.sem, 1)
                            act.wait_ge(k.weights.sem, n)
                            for j in range(q * GRP, (q + 1) * GRP):
                                if j % GRP == 0:
                                    act.wait_ge(k.slot_free.sem,
                                                i * 32 + (s0 + t * 128 + par * 16 + j + GRP))
                                nc.scalar.activation(v.diag[:, j % 8], k.ident[:], ACT.Copy,
                                                     scale=wgt[:, j:j + 1]).then_inc(k.diags.sem, 1)
                            if q == 1:
                                softmax(act, 1 - par, i * 2 + (u0 + t * 8 + par + 1))
                if t >= 1:
                    norm_root(k, act, stats, t - 1)
            norm_root(k, act, stats, NT - 1)

        @block.tensor
        def _(pe):
            if s0 == 0:
                pe.sem_inc(k.slot_free.sem, RING)
            for t in range(NT):
                a = 2 * (t % 2)
                if t >= 2:
                    pe.wait_ge(k.acc_read.sem, k.acc_read.at(t - 1))
                for half in range(2):
                    nc.tensor.matmul(k.ps[:, a + half], k.zeros[:, 0:P], k.zeros[:], start=True, stop=False,
                                     skip_group_check=True)
                with pe.Fori(0, PEER_HEADS // 2) as i:
                    for j in range(2 * TOPK):
                        pe.wait_ge(k.diags.sem, i * 32 + (d0 + t * 128 + j + 1))
                        for half in range(2):
                            mm = nc.tensor.matmul(k.ps[:, a + half], v.diag[:, j % 8],
                                                  v.ring[:, j % RING, D + half * WIDE:D + (half + 1) * WIDE],
                                                  start=False, stop=False, skip_group_check=True)
                        mm.then_inc(k.slot_free.sem, 1)
                for half in range(2):
                    mm = nc.tensor.matmul(k.ps[:, a + half], k.zeros[:, 0:P], k.zeros[:], start=False, stop=True,
                                          skip_group_check=True)
                mm.then_inc(k.acc_ready.sem, 1)

        if last_stage:
            @block.sync
            def _(sp):
                for t in range(NT):
                    sp.wait_ge(k.stored.sem, k.stored.at(t + 1))
                    sp.dma_start(io["out"][t * P:(t + 1) * P], k.res[:, tb + t]).then_inc(k.mods_stored.sem, 16)
                sp.wait_ge(k.mods_stored.sem, 16 + 16 * NT)
    k.slot_free.advance(SEL)
    for x in (k.idx_ready, k.top_ready, k.soft_done):
        x.advance(UNITS + 1)
    for x in k.landed:
        x.advance(16 * ROUNDS)
    k.dots.advance(SEL // GRP)
    k.gelus.advance(SEL // GRP)
    k.weights.advance(SEL // GRP)
    k.diags.advance(SEL)
    for x in (k.acc_ready, k.acc_read, k.var_ready, k.std_ready, k.stored):
        x.advance(NT)


LATENT, CONTEXT = 0, 1


def build(nc, io):
    with ExitStack() as ctx:
        k = setup(nc, ctx, io)
        plan = k.wide_plan
        for layer in range(DEPTH):
            plan += [(layer, W_MOD + b) for b in range(12)]
        for layer in range(DEPTH):
            for stream in (CONTEXT, LATENT):
                full = stream == LATENT or layer < DEPTH - 1
                plan += [(layer, b) for b in range(W_Q if full else W_Z)]
            for stream in (CONTEXT, LATENT):
                if stream == LATENT or layer < DEPTH - 1:
                    plan += [(layer, W_Q + b) for b in range(4)]
        w = stage_mods(k)
        for layer in range(DEPTH):
            last = layer == DEPTH - 1
            for stream in (CONTEXT, LATENT):
                full = stream == LATENT or not last
                w = stage_project(k, layer, stream, w, full)
                stage_states(k, stream)
                if full:
                    stage_outputs(k, stream)
                    w = stage_merge(k, layer, stream, w)
            for stream in (CONTEXT, LATENT):
                if stream == LATENT or not last:
                    w = stage_queries(k, layer, stream, w)
                    stage_retrieve(k, layer, stream, last and stream == LATENT)


def wide_blocks(w):
    n = w.shape[1] // WIDE
    return w.reshape(KT, P, n, WIDE).transpose(2, 1, 0, 3).reshape(n, P, KT * WIDE)


def inverse_counts(length, win):
    t = np.arange(length)
    lo, hi = np.maximum(t - win // 2, 0), np.minimum(t + win - 1 - win // 2, length - 1)
    return (1.0 / (hi - lo + 1)).astype(np.float32)


def kernel(x, c, ctx, c_ctx, w_mod, b_mod, w_in, conv_w, conv_b, a_log, dt_bias, d_skip,
           ssd_norm_g, w_ssd_out, pool_w, pool_scale, w_o, ln_g, ln_b, w_q, sub_keys, u_tab, v_tab):
    import concourse.bacc as bacc
    from concourse.bass_utils import run_bass_kernel_spmd

    A = np.asarray
    w_in = A(w_in)
    wide = np.empty((DEPTH, N_WIDE, P, KT * WIDE), np.float32)
    for l in range(DEPTH):
        wide[l, W_SCAN:W_Z] = wide_blocks(w_in[l, :, 0:COL_DT])
        wide[l, W_Z:W_SSD] = wide_blocks(w_in[l, :, COL_Z:])
        wide[l, W_SSD:W_O] = wide_blocks(A(w_ssd_out)[l])
        wide[l, W_O:W_Q] = wide_blocks(A(w_o)[l])
        wide[l, W_Q:W_MOD] = wide_blocks(A(w_q)[l])
        wide[l, W_MOD:] = wide_blocks(A(w_mod)[l])
    cols = lambda a: A(a).reshape(DEPTH, -1, P).transpose(0, 2, 1)
    taps = A(conv_w).reshape(DEPTH, CONV_W, SCAN_TILES, P).transpose(0, 3, 2, 1).reshape(DEPTH, P, -1)
    grid = [np.outer(inverse_counts(SEQ // GRID_W, w), inverse_counts(GRID_W, w)).reshape(-1) for w in POOL_WINDOWS]
    tri = np.triu(np.ones((P, P), np.float32))
    arrays = {
        "wide": wide,
        "w_dt": w_in[:, :, COL_DT:COL_Z].reshape(DEPTH, KT, P, 32).transpose(0, 2, 1, 3),
        "cvec": np.stack([A(c)[0], A(c_ctx)]).reshape(2, KT, P).transpose(2, 1, 0),
        "b_mod": A(b_mod)[None],
        "tokens": np.concatenate([A(ctx)[0], A(x)[0]]).reshape(6, P, D),
        "pcols": np.concatenate([taps, cols(conv_b), cols(pool_scale), cols(ssd_norm_g)], axis=2),
        "hrows": np.concatenate([A(a_log).reshape(DEPTH, 32), A(dt_bias).reshape(DEPTH, 32), A(d_skip)], axis=1),
        "pool_w": A(pool_w).transpose(0, 2, 1, 3),
        "ln_g": A(ln_g), "ln_b": A(ln_b),
        "keys": A(sub_keys).transpose(0, 4, 1, 2, 3).reshape(DEPTH, P, 16, N_KEYS),
        "experts": np.concatenate([A(u_tab), A(v_tab)], axis=2).reshape(DEPTH * N_EXPERTS, 2 * D),
        "ident": np.eye(P, dtype=np.float32),
        "tri": np.stack([tri, tri.T], axis=1),
        "iota": np.tile(np.arange(TOPK, dtype=np.float32), (P, 1)),
        "icnt_grid": np.stack(grid).astype(np.float32),
        "icnt_line": np.stack([inverse_counts(CTX_LEN, w) for w in POOL_WINDOWS]),
    }
    nc = bacc.Bacc("TRN2", target_bir_lowering=False, num_devices=1)
    io = {}
    for name, a in arrays.items():
        arrays[name] = np.ascontiguousarray(a)
        io[name] = nc.dram_tensor(f"in_{name}", a.shape, F32, kind="ExternalInput").ap()
    io["mods"] = nc.dram_tensor("mod_rows", (DEPTH, 2, 6 * D), F32, kind="Internal").ap()
    io["out"] = nc.dram_tensor("out_x", (SEQ, D), F32, kind="ExternalOutput").ap()
    build(nc, io)
    r = run_bass_kernel_spmd(nc, [{f"in_{n}": a for n, a in arrays.items()}], core_ids=[0])
    return r.results[0]["out_x"].reshape(1, SEQ, D)
```

```python
from contextlib import ExitStack

import numpy as np

import concourse.bass as bass
from concourse import mybir

F32 = mybir.dt.float32
U32 = mybir.dt.uint32
F32R = mybir.dt.float32r
ALU = mybir.AluOpType
ACT = mybir.ActivationFunctionType
AX_X = mybir.AxisListType.X

P = 128
D = 1024
KT = D // P
DEPTH = 2
SEQ, CTX_LEN, GRID_W = 512, 256, 64
ALPHA = (2.0 * DEPTH) ** 0.25
EPS = 1e-6
HEADS, HEAD_DIM, GROUPS = 16, 64, 4
HPG = HEADS // GROUPS
GW = HPG * HEAD_DIM
CONV_W = 5
SCAN_TILES = 16
X_TILES, B_TILES = 8, 4
POOL_WINDOWS = (2, 4, 8, 16)
PEER_HEADS, N_KEYS, TOPK = 8, 128, 16
N_EXPERTS = N_KEYS * N_KEYS
COL_DT, COL_Z = 2048, 2080
COL_POOL = COL_Z + D
BANK = 512
WIDE = 256
PC_CONV, PC_BIAS, PC_SCALE, PC_NORM, PC_N = 0, 80, 96, 104, 112
HR_ALOG, HR_BIAS, HR_SKIP, HR_N = 0, 32, 64, 80
W_SCAN, W_Z, W_POOL, W_GP, W_GS, W_SSD, W_O, W_Q, W_MOD = 0, 8, 12, 14, 18, 22, 26, 30, 38
N_MOD = 6 * D // WIDE
N_WIDE = W_MOD + N_MOD
WIDE_SLOTS = 3
HI_SLOTS = 2
SBUF_FREE = 16512
RING = 8
GRP = 4
PAD = 8
NEG = -3.0e38


A_HT, A_XTOK, A_BT, A_CT, A_BTOK, A_ZS, A_HIN, A_SCR, A_ROWS = 0, 4096, 8192, 10240, 12288, 14336, 18432, 24576, 32000
A_TMP = A_HIN + 4096
ARENA = A_ROWS + PC_N + HR_N + KT * 32 + 16 + 4 * 288


class Bag:
    pass


class Signal:

    def __init__(self, k, name):
        self.sem = k.ctx.enter_context(k.nc.semaphore(name))
        self.base = 0

    def at(self, n):
        return self.base + n

    def advance(self, n):
        self.base += n


def setup(nc, ctx, io):
    k = Bag()
    k.nc, k.ctx, k.io, k.wide_plan, k.wide_next = nc, ctx, io, [], 0
    k.free, k.place = SBUF_FREE, {}

    def sb(name, shape, dt=F32):
        k.place[name] = k.free
        k.free += -(-4 * int(np.prod(shape[1:])) // 32) * 32
        return nc.alloc_sbuf_tensor_at(name, shape, dt, offset=k.place[name])

    def alias(name, shape, other, words=0, dt=F32R):
        return nc.alloc_sbuf_tensor_at(name, shape, dt, offset=k.place[other] + 4 * words)

    k.res = sb("residual", [P, 6, D])
    k.wide = sb("wide_blocks", [P, WIDE_SLOTS, KT, WIDE])
    k.wide_lo = alias("wide_low", [P, WIDE_SLOTS, KT, WIDE], "wide_blocks")
    k.wide_hi = sb("wide_high", [P, HI_SLOTS, KT, WIDE], F32R)
    k.rows = alias("retrieve_rows", [P, 3, D], "wide_high", dt=F32)
    k.ident = sb("identity", [P, P])
    k.tri = sb("triangles", [P, 2, P])
    k.ones = sb("ones", [P, P])
    k.zeros = sb("zeros", [P, BANK])
    k.iota = sb("iota16", [P, TOPK])
    k.eps = sb("eps", [P, 1])
    k.hfin = sb("final_states", [P, 2, D])
    k.arena = sb("arena", [P, ARENA])
    split = lambda name, at: alias(name, [P, KT, SEQ], "arena", at)[:]
    k.act_a = split("activation_a", A_HT)
    k.act_b = split("activation_b", A_XTOK)
    k.act_c = split("activation_c", A_ZS)
    k.act_d = split("activation_d", A_HIN)
    k.act_e = split("activation_e", A_BT)
    k.ps = ctx.enter_context(nc.psum_tensor("banks", [P, 8, BANK], F32))
    k.loaded = Signal(k, "loaded")
    k.mod_ready = Signal(k, "mod_ready")
    k.mod_used = Signal(k, "mod_used")
    k.mods_stored = Signal(k, "mods_stored")
    k.wide_used = Signal(k, "wide_used")
    k.xt_ready = Signal(k, "xt_ready")
    k.h_hi = Signal(k, "h_hi")
    k.h_ready = Signal(k, "h_ready")
    k.wide_rounded = Signal(k, "wide_rounded")
    k.wide_cut = Signal(k, "wide_cut")
    k.y_hi = Signal(k, "y_hi")
    k.merged_hi = Signal(k, "merged_hi")
    k.merged_lo = Signal(k, "merged_lo")
    k.h2_hi = Signal(k, "h2_hi")
    k.proj_ready = Signal(k, "proj_ready")
    k.padded = Signal(k, "padded")
    k.conv_ready = Signal(k, "conv_ready")
    k.silu_done = Signal(k, "silu_done")
    k.turned = Signal(k, "turned")
    k.turn_copied = Signal(k, "turn_copied")
    k.dt_proj = Signal(k, "dt_proj")
    k.dt_copied = Signal(k, "dt_copied")
    k.z_proj = Signal(k, "z_proj")
    k.z_done = Signal(k, "z_done")
    k.consts_set = Signal(k, "consts_set")
    k.dt_vec = Signal(k, "dt_vec")
    k.dt_act = Signal(k, "dt_act")
    k.cum_ready = Signal(k, "cum_ready")
    k.xs_ready = Signal(k, "xs_ready")
    k.state_ready = Signal(k, "state_ready")
    k.state_added = Signal(k, "state_added")
    k.cb_ready = Signal(k, "cb_ready")
    k.cb_masked = Signal(k, "cb_masked")
    k.dtab_ready = Signal(k, "dtab_ready")
    k.acum_ready = Signal(k, "acum_ready")
    k.seg_ready = Signal(k, "seg_ready")
    k.m_ready = Signal(k, "m_ready")
    k.group_summed = Signal(k, "group_summed")
    k.y_ready = Signal(k, "y_ready")
    k.y_read = Signal(k, "y_read")
    k.inter_ready = Signal(k, "inter_ready")
    k.inter_read = Signal(k, "inter_read")
    k.gated = Signal(k, "gated")
    k.xd_ready = Signal(k, "xd_ready")
    k.rms_ready = Signal(k, "rms_ready")
    k.yn_ready = Signal(k, "yn_ready")
    k.yt_turned = Signal(k, "yt_turned")
    k.yt_copied = Signal(k, "yt_copied")
    k.pin_proj = Signal(k, "pin_proj")
    k.pin_copied = Signal(k, "pin_copied")
    k.mixed_ready = Signal(k, "mixed_ready")
    k.gp_proj = Signal(k, "gp_proj")
    k.gp_sig = Signal(k, "gp_sig")
    k.yp_proj = Signal(k, "yp_proj")
    k.merged0 = Signal(k, "merged0")
    k.gs_proj = Signal(k, "gs_proj")
    k.gs_sig = Signal(k, "gs_sig")
    k.ys_proj = Signal(k, "ys_proj")
    k.merged1 = Signal(k, "merged1")
    k.mix_proj = Signal(k, "mix_proj")
    k.mix_read = Signal(k, "mix_read")
    k.var_ready = Signal(k, "var_ready")
    k.std_ready = Signal(k, "std_ready")
    k.h2_ready = Signal(k, "h2_ready")
    k.h2_turned = Signal(k, "h2_turned")
    k.h2_copied = Signal(k, "h2_copied")
    k.q_proj = Signal(k, "q_proj")
    k.q_copied = Signal(k, "q_copied")
    k.s_proj = Signal(k, "s_proj")
    k.s_copied = Signal(k, "s_copied")
    k.idx_ready = Signal(k, "idx_ready")
    k.dots = Signal(k, "dots")
    k.gelus = Signal(k, "gelus")
    k.weights = Signal(k, "weights")
    k.diags = Signal(k, "diags")
    k.slot_free = Signal(k, "slot_free")
    k.acc_ready = Signal(k, "acc_ready")
    k.acc_read = Signal(k, "acc_read")
    k.top_ready = Signal(k, "top_ready")
    k.soft_done = Signal(k, "soft_done")
    k.pool_steps = Signal(k, "pool_steps")
    k.stored = Signal(k, "stored")
    k.decay_ready = Signal(k, "decay_ready")
    k.wide_landed = [Signal(k, f"wide_landed{i}") for i in range(WIDE_SLOTS)]
    k.landed = [Signal(k, f"row_landed{i}") for i in range(RING)]
    return k


def carve(k, *sizes):
    out, at = [], 0
    for words in sizes:
        out.append(k.arena[:, at:at + words])
        at += words
    assert at <= k.arena.shape[1], (at, k.arena.shape)
    return out


def bc(ap, shape):
    return ap.unsqueeze(2).to_broadcast(shape)


def load_wides(k, sp, upto):
    upto = min(upto, len(k.wide_plan))
    while k.wide_next < upto:
        n = k.wide_next
        layer, block = k.wide_plan[n]
        if n >= WIDE_SLOTS:
            sp.wait_ge(k.wide_used.sem, n - WIDE_SLOTS + 1)
        sp.dma_start(k.wide[:, n % WIDE_SLOTS].rearrange("p t c -> p (t c)"),
                     k.io["wide"][layer, block]).then_inc(k.wide_landed[n % WIDE_SLOTS].sem, 16)
        k.wide_next += 1


def round_wides(k, act, last):
    while k.next_round <= last:
        n = k.next_round
        act.wait_ge(k.wide_landed[n % WIDE_SLOTS].sem, 16 * (n // WIDE_SLOTS + 1))
        if n - k.cut0 >= HI_SLOTS:
            act.wait_ge(k.wide_used.sem, n - HI_SLOTS + 1)
        k.nc.scalar.copy(k.wide_hi[:, n % HI_SLOTS], k.wide[:, n % WIDE_SLOTS]).then_inc(k.wide_rounded.sem, 1)
        k.next_round += 1


def cut_wides(k, pool, last):
    for n in range(k.next_cut, last + 1):
        pool.wait_ge(k.wide_rounded.sem, n - k.cut0 + 1)
        k.nc.gpsimd.tensor_tensor(k.wide_lo[:, n % WIDE_SLOTS], k.wide[:, n % WIDE_SLOTS],
                                  k.wide_hi[:, n % HI_SLOTS].bitcast(F32), ALU.subtract) \
            .then_inc(k.wide_cut.sem, 1)
    k.next_cut = last + 1


def take_wide(k, pe, n):
    pe.wait_ge(k.wide_cut.sem, n - k.cut0 + 1)
    return k.wide_hi[:, n % HI_SLOTS], k.wide_lo[:, n % WIDE_SLOTS]


def product(nc, out, lhs, rhs, ready=None):
    for kt in range(KT):
        if ready:
            ready(kt)
        (lh, ll), (rh, rl) = lhs(kt), rhs(kt)
        nc.tensor.matmul(out, lh, rh, start=(kt == 0), stop=False)
        nc.tensor.matmul(out, lh, rl, start=False, stop=False)
        last = nc.tensor.matmul(out, ll, rh, start=False, stop=(kt == KT - 1))
    return last


def turn_tokens(k, pe, NT, tb):
    for kt in range(KT):
        if kt >= 2:
            pe.wait_ge(k.h_hi.sem, k.h_hi.at(kt - 1))
        for t in range(NT):
            last = k.nc.tensor.transpose(k.ps[:, kt % 2, t * P:(t + 1) * P],
                                         k.res[:, tb + t, kt * P:(kt + 1) * P], k.ident[:])
        last.then_inc(k.xt_ready.sem, 1)


def modulate(k, act, v, T):
    for kt in range(KT):
        act.wait_ge(k.xt_ready.sem, k.xt_ready.at(kt + 1))
        if kt >= 2:
            act.wait_ge(k.h_ready.sem, k.h_ready.at(kt - 1))
        for dst, sig in ((k.act_a[:, kt, 0:T], None), (v.hraw[:, kt % 2, 0:T], k.h_hi)):
            op = k.nc.scalar.activation(dst, k.ps[:, kt % 2, 0:T], ACT.Identity,
                                        bias=v.modc[:, 0, kt:kt + 1], scale=v.modc[:, 1, kt:kt + 1])
            if sig:
                op.then_inc(sig.sem, 1)


def modulate_rest(k, dve, v, low, T):
    for kt in range(KT):
        dve.wait_ge(k.h_hi.sem, k.h_hi.at(kt + 1))
        k.nc.vector.tensor_tensor(low[:, kt, 0:T], v.hraw[:, kt % 2, 0:T], k.act_a[:, kt, 0:T].bitcast(F32),
                                  ALU.subtract).then_inc(k.h_ready.sem, 1)


def stage_mods(k):
    nc, io = k.nc, k.io
    cvec, csil, brow = carve(k, KT * 2, KT * 2, DEPTH * 6 * D)
    cvec = cvec.rearrange("p (t s) -> p t s", s=2)
    csil = csil.rearrange("p (t s) -> p t s", s=2)
    brow = brow.rearrange("p (l c) -> p l c", l=DEPTH)
    n_blk = DEPTH * N_MOD

    with nc.Block() as block:
        @block.sync
        def _(sp):
            for dst, src in ((cvec, io["cvec"]), (k.ident[:], io["ident"]), (k.tri[:], io["tri"]), (k.iota[:], io["iota"]),
                             (brow[0:1], io["b_mod"]), (brow[1:2], io["b_mod"])):
                sp.dma_start(dst, src).then_inc(k.loaded.sem, 16)
            load_wides(k, sp, WIDE_SLOTS)
            for t in range(6):
                sp.dma_start(k.res[:, t], io["tokens"][t]).then_inc(k.loaded.sem, 16)
            load_wides(k, sp, n_blk + WIDE_SLOTS)
            sp.wait_ge(k.mod_used.sem, n_blk)
            sp.dma_start(io["mods"].rearrange("l s c -> s l c"), brow[0:2]).then_inc(k.mods_stored.sem, 16)
            sp.wait_ge(k.mods_stored.sem, 16)
            sp.wait_ge(k.loaded.sem, 12 * 16)

        @block.scalar
        def _(act):
            act.wait_ge(k.loaded.sem, 12 * 16)
            nc.scalar.activation(csil, cvec, ACT.Silu).then_inc(k.h_ready.sem, 1)

        @block.gpsimd
        def _(pool):
            pool.memset(k.ones[:], 1.0)
            pool.memset(k.zeros[:], 0.0)
            pool.memset(k.eps[:], EPS).then_inc(k.consts_set.sem, 1)

        @block.tensor
        def _(pe):
            pe.wait_ge(k.h_ready.sem, 1)
            for n in range(n_blk):
                slot = n % WIDE_SLOTS
                pe.wait_ge(k.wide_landed[slot].sem, 16 * (n // WIDE_SLOTS + 1))
                if n >= 2:
                    pe.wait_ge(k.mod_used.sem, n - 1)
                for kt in range(KT):
                    last = nc.tensor.matmul(k.ps[0:2, n % 2, 0:WIDE], csil[:, kt], k.wide[:, slot, kt],
                                            start=(kt == 0), stop=(kt == KT - 1))
                last.then_inc(k.mod_ready.sem, 1)
                pe.drain().then_inc(k.wide_used.sem, 1)

        @block.vector
        def _(dve):
            dve.wait_ge(k.loaded.sem, 12 * 16)
            for n in range(n_blk):
                row = brow[0:2, n // N_MOD, (n % N_MOD) * WIDE:(n % N_MOD + 1) * WIDE]
                dve.wait_ge(k.mod_ready.sem, n + 1)
                nc.vector.tensor_tensor(row, k.ps[0:2, n % 2, 0:WIDE], row, ALU.add).then_inc(k.mod_used.sem, 1)
    k.loaded.advance(12 * 16)
    k.h_ready.advance(1)
    k.cut0 = k.next_round = k.next_cut = n_blk
    k.consts_set.advance(1)
    return n_blk


def mixer_views(k):
    v = Bag()
    (_, xtok, BT, CT, Btok, zs, hin, scr, pcols, hrow, wdt, modc, dts) = carve(
        k, 8 * 512, 4 * D, 4 * 512, 4 * 512, 4 * 512, 4 * D, 6 * D, A_ROWS - A_SCR, PC_N, HR_N, KT * 32, 16, 4 * 288)
    r = lambda ap, n: ap.rearrange("p (a b) -> p a b", a=n)
    v.xtok, v.BT, v.CT, v.Btok, v.zs = (r(xtok, 4), r(BT, 4), r(CT, 4), r(Btok, 4), r(zs, 4))
    v.hraw = r(k.arena[:, A_TMP:A_TMP + 2 * SEQ], 2)
    v.hin = hin.rearrange("p (d c e) -> p d c e", d=2, c=3)
    v.pcols, v.hrow, v.wdt, v.modc = pcols, hrow, r(wdt, KT), r(modc, 2)
    v.scr = scr
    v.raw_hin = hin
    v.dt, v.dta, v.e32, v.eac, v.dte, v.tmp32 = (r(dts[:, i * 128:(i + 1) * 128], 4) for i in range(6))
    v.cum = r(dts[:, 768:768 + 256], 4)
    v.ctot = r(dts[:, 1024:1024 + 128], 4)
    return v


def stage_project(k, layer, stream, w0, full):
    nc, io = k.nc, k.io
    T = SEQ if stream == 0 else CTX_LEN
    NT, tb = T // P, (2 if stream == 0 else 0)
    v = mixer_views(k)
    upad = v.scr[:, 0:2 * 520].rearrange("p (a b) -> p a b", a=2)
    acc = v.scr[:, 1040:1040 + 1024].rearrange("p (a b) -> p a b", a=2)
    sx = v.scr[:, 2064:2064 + 1024].rearrange("p (a b) -> p a b", a=2)
    mods = io["mods"][layer, stream]
    n_wide = 12 if full else 8
    hT = lambda kt, cut=slice(0, T): (k.act_a[:, kt, cut], k.act_d[:, kt, cut])
    ld = k.loaded.base
    zg = 4 * NT if full else 0

    def sx_or_bt(m):
        if m < X_TILES:
            return sx[:, m % 2, 0:T]
        if m < X_TILES + B_TILES:
            return v.BT[:, m - X_TILES, 0:T]
        return v.CT[:, m - X_TILES - B_TILES, 0:T]

    with nc.Block() as block:
        @block.sync
        def _(sp):
            sp.dma_start(v.modc, mods[0:2 * D].rearrange("(a t p) -> p a t", a=2, p=P),
                         allow_slow_non_contiguous=True).then_inc(k.loaded.sem, 16)
            sp.dma_start(v.pcols, io["pcols"][layer]).then_inc(k.loaded.sem, 16)
            sp.dma_start(v.hrow, io["hrows"][layer:layer + 1].to_broadcast([P, HR_N])).then_inc(k.loaded.sem, 16)
            sp.dma_start(v.wdt, io["w_dt"][layer]).then_inc(k.loaded.sem, 16)
            load_wides(k, sp, w0 + n_wide + WIDE_SLOTS)
            sp.wait_ge(k.loaded.sem, ld + 64)

        @block.tensor
        def _(pe):
            turn_tokens(k, pe, NT, tb)

            def turn(m):
                src = sx_or_bt(m)
                pe.wait_ge(k.silu_done.sem, k.silu_done.at(m + 1))
                if m >= 2:
                    pe.wait_ge(k.turn_copied.sem, k.turn_copied.at(m - 1))
                for t in range(NT):
                    last = nc.tensor.transpose(k.ps[:, 4 + m % 2, t * P:(t + 1) * P],
                                               src[:, t * P:(t + 1) * P], k.ident[:])
                last.then_inc(k.turned.sem, 1)

            for m in range(SCAN_TILES):
                wh, wl = take_wide(k, pe, w0 + m // 2)
                if m >= 2:
                    pe.wait_ge(k.padded.sem, k.padded.at(m - 1))
                cut = slice((m % 2) * P, (m % 2 + 1) * P)
                product(nc, k.ps[:, 2 + m % 2, 0:T], lambda kt: (wh[:, kt, cut], wl[:, kt, cut]), hT,
                        ready=(lambda kt: pe.wait_ge(k.h_ready.sem, k.h_ready.at(kt + 1))) if m == 0 else None) \
                    .then_inc(k.proj_ready.sem, 1)
                if m % 2 == 1:
                    pe.drain().then_inc(k.wide_used.sem, 1)
                if 2 <= m < 2 + X_TILES + B_TILES:
                    turn(m - 2)
            pe.wait_ge(k.loaded.sem, ld + 64)
            for t in range(NT):
                for n in range(2 * KT):
                    part = hT(n // 2, slice(t * P, (t + 1) * P))[n % 2]
                    last = nc.tensor.matmul(k.ps[:, 6, t * 32:(t + 1) * 32], part.bitcast(F32), v.wdt[:, n // 2],
                                            start=(n == 0), stop=(n == 2 * KT - 1))
            last.then_inc(k.dt_proj.sem, 1)
            pe.wait_ge(k.padded.sem, k.padded.at(SCAN_TILES))
            for n in range(zg):
                wh, wl = take_wide(k, pe, w0 + 8 + n // NT)
                if n >= 2:
                    pe.wait_ge(k.z_done.sem, k.z_done.at(n - 1))
                t = n % NT
                product(nc, k.ps[:, 2 + n % 2, 0:WIDE], lambda kt: hT(kt, slice(t * P, (t + 1) * P)),
                        lambda kt: (wh[:, kt], wl[:, kt])).then_inc(k.z_proj.sem, 1)
                if t == NT - 1:
                    pe.drain().then_inc(k.wide_used.sem, 1)

        @block.scalar
        def _(act):
            act.wait_ge(k.loaded.sem, ld + 64)
            act.wait_ge(k.consts_set.sem, k.consts_set.at(1))
            round_wides(k, act, w0)
            modulate(k, act, v, T)
            round_wides(k, act, w0 + 1)
            for m in range(SCAN_TILES + 1):
                if m % 2 == 0 and 2 <= m:
                    round_wides(k, act, w0 + m // 2 + 1)
                if m < SCAN_TILES:
                    act.wait_ge(k.proj_ready.sem, k.proj_ready.at(m + 1))
                    if m >= 2:
                        act.wait_ge(k.conv_ready.sem, k.conv_ready.at(m - 1))
                    nc.scalar.copy(upad[:, m % 2, 2:2 + T], k.ps[:, 2 + m % 2, 0:T]).then_inc(k.padded.sem, 1)
                if m >= 1:
                    act.wait_ge(k.conv_ready.sem, k.conv_ready.at(m))
                    if 2 < m <= X_TILES:
                        act.wait_ge(k.turned.sem, k.turned.at(m - 2))
                    nc.scalar.activation(sx_or_bt(m - 1), acc[:, (m - 1) % 2, 0:T], ACT.Silu,
                                         bias=v.pcols[:, PC_BIAS + m - 1:PC_BIAS + m]).then_inc(k.silu_done.sem, 1)
            act.wait_ge(k.dt_proj.sem, k.dt_proj.at(1))
            nc.scalar.copy(v.dt[:, 0:NT], k.ps[:, 6, 0:NT * 32].rearrange("p (t c) -> p t c", c=32)) \
                .then_inc(k.dt_copied.sem, 1)
            for n in range(zg):
                if n % NT == 0 and n >= NT:
                    round_wides(k, act, w0 + 8 + n // NT + 1)
                act.wait_ge(k.z_proj.sem, k.z_proj.at(n + 1))
                nc.scalar.activation(v.zs[:, n % NT, (n // NT) * WIDE:(n // NT + 1) * WIDE],
                                     k.ps[:, 2 + n % 2, 0:WIDE], ACT.Silu).then_inc(k.z_done.sem, 1)
            round_wides(k, act, w0 + n_wide + 1)

        @block.gpsimd
        def _(pool):
            cut_wides(k, pool, w0 + n_wide + 1)

        @block.vector
        def _(dve):
            nc.vector.memset(upad, 0.0)
            dve.wait_ge(k.loaded.sem, ld + 64)
            nc.vector.tensor_scalar(v.modc[:, 1], v.modc[:, 1], 1.0, None, ALU.add).then_inc(k.consts_set.sem, 1)

            modulate_rest(k, dve, v, k.act_d, T)

            def copy_turned(m):
                dve.wait_ge(k.turned.sem, k.turned.at(m + 1))
                dst = (v.xtok[:, 0:NT, m * P:(m + 1) * P] if m < X_TILES
                       else v.Btok[:, 0:NT, (m - X_TILES) * P:(m - X_TILES + 1) * P])
                nc.vector.tensor_copy(dst, k.ps[:, 4 + m % 2, 0:T].rearrange("p (t c) -> p t c", c=P)) \
                    .then_inc(k.turn_copied.sem, 1)

            for m in range(SCAN_TILES):
                dve.wait_ge(k.padded.sem, k.padded.at(m + 1))
                if m >= 2:
                    dve.wait_ge(k.silu_done.sem, k.silu_done.at(m - 1))
                a = acc[:, m % 2, 0:T]
                for j in range(CONV_W):
                    tap = v.pcols[:, PC_CONV + m * CONV_W + j:PC_CONV + m * CONV_W + j + 1]
                    u = upad[:, m % 2, j:j + T]
                    if j == 0:
                        last = nc.vector.tensor_scalar(a, u, tap, None, ALU.mult)
                    else:
                        dve.drain()
                        last = nc.vector.scalar_tensor_tensor(a, u, tap, a, ALU.mult, ALU.add)
                last.then_inc(k.conv_ready.sem, 1)
                if 2 <= m < 2 + X_TILES + B_TILES:
                    copy_turned(m - 2)
    k.loaded.advance(64)
    k.consts_set.advance(1)
    for s in (k.xt_ready, k.h_hi, k.h_ready):
        s.advance(KT)
    for s in (k.proj_ready, k.padded, k.conv_ready, k.silu_done):
        s.advance(SCAN_TILES)
    for s in (k.turned, k.turn_copied):
        s.advance(X_TILES + B_TILES)
    for s in (k.dt_proj, k.dt_copied):
        s.advance(1)
    for s in (k.z_proj, k.z_done):
        s.advance(zg)
    return w0 + n_wide


def stage_states(k, stream):
    nc = k.nc
    T = SEQ if stream == 0 else CTX_LEN
    NT = T // P
    v = mixer_views(k)
    xs = v.scr[:, 0:2 * D].rearrange("p (a b) -> p a b", a=2)
    hsum = v.scr[:, 2 * D:3 * D]
    ctx = stream == 1
    steps = [(d, t, o) for d in range(2)
             for o, t in enumerate(range(NT) if d == 0 else reversed(range(NT)))
             if ctx or o < NT - 1]

    with nc.Block() as block:
        @block.vector
        def _(dve):
            dt, nt = v.dt[:, 0:NT], slice(0, NT)
            bias = v.hrow[:, HR_BIAS:HR_BIAS + 32].unsqueeze(1).to_broadcast([P, NT, 32])
            nc.vector.tensor_tensor(dt, dt, bias, ALU.add)
            dve.drain()
            nc.vector.scalar_tensor_tensor(v.e32[:, nt], dt, -1.0, dt, ALU.mult, ALU.min).then_inc(k.dt_vec.sem, 1)
            dve.wait_ge(k.dt_act.sem, k.dt_act.at(1))
            nc.vector.scalar_tensor_tensor(dt, dt, 0.0, v.tmp32[:, nt], ALU.max, ALU.add)
            dve.drain()
            ea = v.hrow[:, HR_ALOG:HR_ALOG + 32].unsqueeze(1).to_broadcast([P, NT, 32])
            nc.vector.scalar_tensor_tensor(v.dta[:, nt], dt, -1.0, ea, ALU.mult, ALU.mult).then_inc(k.dt_vec.sem, 1)
            dve.wait_ge(k.cum_ready.sem, k.cum_ready.at(1))
            nc.vector.tensor_copy(v.cum[:, nt], k.ps[:, 0, 0:NT * 64].rearrange("p (t c) -> p t c", c=64))
            dve.drain()
            nc.vector.tensor_tensor(v.e32[:, nt], v.cum[:, nt, 32:64], v.cum[:, nt, 0:32], ALU.subtract) \
                .then_inc(k.dt_vec.sem, 1)
            dve.wait_ge(k.dt_act.sem, k.dt_act.at(2))
            nc.vector.tensor_tensor(v.dte[:, nt], v.tmp32[:, nt], dt, ALU.mult)
            dve.drain()
            heads = lambda ap: ap.rearrange("p (h e) -> p h e", h=HEADS)

            def scale_x(n):
                d, t, _ = steps[n]
                if n >= 2:
                    dve.wait_ge(k.state_ready.sem, k.state_ready.at(n - 1))
                nc.vector.tensor_tensor(heads(xs[:, n % 2]), heads(v.xtok[:, t]),
                                        bc(v.dte[:, t, d * 16:d * 16 + 16], [P, HEADS, HEAD_DIM]), ALU.mult) \
                    .then_inc(k.xs_ready.sem, 1)

            scale_x(0)
            for n, (d, t, o) in enumerate(steps):
                if n + 1 < len(steps):
                    scale_x(n + 1)
                final = o == NT - 1
                dst = k.hfin[:, d] if final else v.hin[:, d, o]
                src = (k.hfin[:, d] if not ctx else None) if o == 0 else v.hin[:, d, o - 1]
                if src is not None:
                    nc.vector.tensor_tensor(heads(hsum), heads(src),
                                            bc(v.ctot[:, t, d * 16:d * 16 + 16], [P, HEADS, HEAD_DIM]), ALU.mult)
                    dve.drain()
                dve.wait_ge(k.state_ready.sem, k.state_ready.at(n + 1))
                st = k.ps[:, 2 + 2 * (n % 2):4 + 2 * (n % 2)].rearrange("p a b -> p (a b)")
                if src is not None:
                    last = nc.vector.tensor_tensor(dst, hsum, st, ALU.add)
                else:
                    last = nc.vector.tensor_copy(dst, st)
                last.then_inc(k.state_added.sem, 1)
                dve.drain()

        @block.scalar
        def _(act):
            nt = slice(0, NT)
            act.wait_ge(k.dt_vec.sem, k.dt_vec.at(1))
            nc.scalar.activation(v.e32[:, nt], v.e32[:, nt], ACT.Exp)
            nc.scalar.activation(v.hrow[:, HR_ALOG:HR_ALOG + 32], v.hrow[:, HR_ALOG:HR_ALOG + 32], ACT.Exp)
            act.drain()
            nc.scalar.activation(v.tmp32[:, nt], v.e32[:, nt], ACT.Ln, bias=k.ones[:, 0:1]).then_inc(k.dt_act.sem, 1)
            act.wait_ge(k.dt_vec.sem, k.dt_vec.at(3))
            nc.scalar.activation(v.tmp32[:, nt], v.e32[:, nt], ACT.Exp)
            nc.scalar.activation(v.eac[:, nt], v.cum[:, nt, 0:32], ACT.Exp)
            nc.scalar.activation(v.ctot[:, nt], v.cum[:, nt, 32:64], ACT.Exp).then_inc(k.dt_act.sem, 1)

        @block.tensor
        def _(pe):
            pe.wait_ge(k.dt_vec.sem, k.dt_vec.at(2))
            for t in range(NT):
                for d in range(2):
                    nc.tensor.matmul(k.ps[:, 0, t * 64 + d * 16:t * 64 + d * 16 + 16], k.tri[:, d],
                                     v.dta[:, t, d * 16:d * 16 + 16], start=True, stop=True)
                last = nc.tensor.matmul(k.ps[:, 0, t * 64 + 32:t * 64 + 64], k.ones[:], v.dta[:, t],
                                        start=True, stop=True)
            last.then_inc(k.cum_ready.sem, 1)
            for n, (d, t, o) in enumerate(steps):
                pe.wait_ge(k.xs_ready.sem, k.xs_ready.at(n + 1))
                if n >= 2:
                    pe.wait_ge(k.state_added.sem, k.state_added.at(n - 1))
                for g in range(GROUPS):
                    last = nc.tensor.matmul(k.ps[:, 2 + 2 * (n % 2) + g // 2, (g % 2) * GW:(g % 2 + 1) * GW],
                                            v.Btok[:, t, g * P:(g + 1) * P], xs[:, n % 2, g * GW:(g + 1) * GW],
                                            start=True, stop=True)
                last.then_inc(k.state_ready.sem, 1)
    k.dt_vec.advance(3)
    k.dt_act.advance(2)
    k.cum_ready.advance(1)
    for s in (k.xs_ready, k.state_ready, k.state_added):
        s.advance(len(steps))


def stage_outputs(k, stream):
    nc = k.nc
    T = SEQ if stream == 0 else CTX_LEN
    NT = T // P
    ctx = stream == 1
    v = mixer_views(k)
    s = v.scr
    cbm = s[:, 0:1024].rearrange("p (d c) -> p d c", d=2)
    dtab = s[:, 1024:3072].rearrange("p (a h c) -> p a h c", a=4, h=HPG)
    m_buf = s[:, 3072:5120].rearrange("p (a h c) -> p a h c", a=4, h=HPG)
    xd = k.arena[:, A_HT:A_HT + 4 * D].rearrange("p (a d c) -> p a d c", a=2, d=2)
    ysum = s[:, 5120:5120 + D]
    ytmp = s[:, 6144:6144 + D]
    sq = s[:, 7168:7168 + 256]
    ss = v.e32[:, :, 0:GROUPS]
    heads = lambda ap: ap.rearrange("p (h e) -> p h e", h=HEADS)
    units = [(t, d, g) for t in range(NT) for d in range(2) for g in range(GROUPS)]
    order = lambda d, t: t if d == 0 else NT - 1 - t
    inters = [(t, d) for t in range(NT) for d in range(2) if not (ctx and order(d, t) == 0)]
    per = 2 * GROUPS
    Y, INT, CB = 2, 4, 6
    SUMS = (0, 1, 7)
    LAG = 2

    with nc.Block() as block:
        @block.gpsimd
        def _(pool):
            def scale_x(t):
                if t >= 2:
                    pool.wait_ge(k.y_ready.sem, k.y_ready.at(t - 1))
                for dd in range(2):
                    pool.tensor_tensor(heads(xd[:, t % 2, dd]), heads(v.xtok[:, t]),
                                       bc(v.dt[:, t, dd * 16:dd * 16 + 16], [P, HEADS, HEAD_DIM]), ALU.mult) \
                        .then_inc(k.xd_ready.sem, 1)

            for n, (t, d, g) in enumerate(units):
                if n >= 4:
                    pool.wait_ge(k.acum_ready.sem, k.acum_ready.at(n - 3))
                h0 = d * 16 + g * HPG
                pool.tensor_copy(dtab[:, n % 4], bc(v.dta[:, t, h0:h0 + HPG], [P, HPG, P])) \
                    .then_inc(k.dtab_ready.sem, 1)
                if n == 0:
                    scale_x(0)
                if g == 0 and d == 1 and t + 1 < NT:
                    scale_x(t + 1)

        @block.tensor
        def _(pe):
            def intra(n):
                t, d, g = units[n]
                pe.wait_ge(k.m_ready.sem, k.m_ready.at(n + 1))
                pe.wait_ge(k.xd_ready.sem, k.xd_ready.at(2 * t + 2))
                if d == 0 and g == 0 and t >= 1:
                    pe.wait_ge(k.y_read.sem, k.y_read.at(t))
                for h in range(HPG):
                    hh = g * HPG + h
                    last = nc.tensor.matmul(k.ps[:, Y + g // 2, (hh % 8) * HEAD_DIM:(hh % 8 + 1) * HEAD_DIM],
                                            m_buf[:, n % 4, h], xd[:, t % 2, d, hh * HEAD_DIM:(hh + 1) * HEAD_DIM],
                                            start=(d == 0 and hh % 8 == 0), stop=(d == 1 and hh % 8 == 7),
                                            skip_group_check=True)
                last.then_inc(k.y_ready.sem if g == GROUPS - 1 and d == 1 else k.group_summed.sem, 1)

            for n, (t, d, g) in enumerate(units):
                if d == 0 and g == 0:
                    if t >= 1:
                        pe.wait_ge(k.cb_masked.sem, k.cb_masked.at(t))
                    for gg in range(GROUPS):
                        last = nc.tensor.matmul(k.ps[:, CB, gg * P:(gg + 1) * P], v.BT[:, gg, t * P:(t + 1) * P],
                                                v.CT[:, gg, t * P:(t + 1) * P], start=True, stop=True)
                    last.then_inc(k.cb_ready.sem, 1)
                pe.wait_ge(k.dtab_ready.sem, k.dtab_ready.at(n + 1))
                if n >= 3:
                    pe.wait_ge(k.seg_ready.sem, k.seg_ready.at(n - 2))
                for h in range(HPG):
                    last = nc.tensor.matmul(k.ps[:, SUMS[n % 3], h * P:(h + 1) * P], dtab[:, n % 4, h], k.tri[:, d],
                                            start=True, stop=True)
                last.then_inc(k.acum_ready.sem, 1)
                if n >= LAG:
                    intra(n - LAG)
                if g == 2 and (t, d) in inters:
                    i = inters.index((t, d))
                    if i >= 1:
                        pe.wait_ge(k.inter_read.sem, k.inter_read.at(i))
                    o = order(d, t)
                    h_in = k.hfin[:, d] if o == 0 else v.hin[:, d, o - 1]
                    for gg in range(GROUPS):
                        last = nc.tensor.matmul(k.ps[:, INT + gg // 2, (gg % 2) * GW:(gg % 2 + 1) * GW],
                                                v.CT[:, gg, t * P:(t + 1) * P], h_in[:, gg * GW:(gg + 1) * GW],
                                                start=True, stop=True)
                    last.then_inc(k.inter_ready.sem, 1)
            for n in range(len(units) - LAG, len(units)):
                intra(n)

        @block.scalar
        def _(act):
            def squares(t):
                act.wait_ge(k.gated.sem, k.gated.at(t + 1))
                for g in range(GROUPS):
                    nc.scalar.activation(sq, v.zs[:, t, g * GW:(g + 1) * GW], ACT.Square,
                                         accum_out=ss[:, t, g:g + 1])
                    act.drain()

            for n, (t, d, g) in enumerate(units):
                act.wait_ge(k.acum_ready.sem, k.acum_ready.at(n + 1))
                if n >= 4:
                    tt, dd, gg = units[n - 4]
                    if (dd, gg) == (1, GROUPS - 1):
                        act.wait_ge(k.y_ready.sem, k.y_ready.at(tt + 1))
                    else:
                        act.wait_ge(k.group_summed.sem, k.group_summed.at(n - 3 - tt))
                for h in range(HPG):
                    col = d * 16 + g * HPG + h
                    last = nc.scalar.activation(m_buf[:, n % 4, h], k.ps[:, SUMS[n % 3], h * P:(h + 1) * P], ACT.Relu,
                                                bias=v.cum[:, t, col:col + 1], scale=-1.0)
                last.then_inc(k.seg_ready.sem, 1)
                act.drain()
                nc.scalar.activation(m_buf[:, n % 4], m_buf[:, n % 4], ACT.Exp, scale=-1.0) \
                    .then_inc(k.decay_ready.sem, 1)
                if (d, g) == (0, 3) and t >= 1:
                    squares(t - 1)
            squares(NT - 1)

        @block.vector
        def _(dve):
            def gate(t):
                dve.wait_ge(k.y_ready.sem, k.y_ready.at(t + 1))
                dve.drain()
                nc.vector.tensor_tensor(ysum, ysum, k.ps[:, Y:Y + 2].rearrange("p a b -> p (a b)"), ALU.add) \
                    .then_inc(k.y_read.sem, 1)
                dve.drain()
                nc.vector.tensor_tensor(v.zs[:, t], v.zs[:, t], ysum, ALU.mult).then_inc(k.gated.sem, 1)

            for n, (t, d, g) in enumerate(units):
                if d == 0 and g == 0:
                    dve.wait_ge(k.cb_ready.sem, k.cb_ready.at(t + 1))
                    cb = k.ps[:, CB].rearrange("p (g c) -> p g c", g=GROUPS)
                    for dd in range(2):
                        last = nc.vector.tensor_tensor(cbm[:, dd].rearrange("p (g c) -> p g c", g=GROUPS), cb,
                                                       k.tri[:, dd].unsqueeze(1).to_broadcast([P, GROUPS, P]),
                                                       ALU.mult)
                    last.then_inc(k.cb_masked.sem, 1)
                    dve.drain()
                dve.wait_ge(k.decay_ready.sem, k.decay_ready.at(n + 1))
                nc.vector.tensor_tensor(m_buf[:, n % 4], m_buf[:, n % 4],
                                        cbm[:, d, g * P:(g + 1) * P].unsqueeze(1).to_broadcast([P, HPG, P]),
                                        ALU.mult).then_inc(k.m_ready.sem, 1)
                if g == LAG - 1 and d == 0:
                    if t >= 1:
                        gate(t - 1)
                        dve.drain()
                    nc.vector.tensor_tensor(heads(ysum), heads(v.xtok[:, t]),
                                            bc(v.hrow[:, HR_SKIP:HR_SKIP + 16], [P, HEADS, HEAD_DIM]), ALU.mult)
                if g == 3 and (t, d) in inters:
                    i = inters.index((t, d))
                    dve.wait_ge(k.inter_ready.sem, k.inter_ready.at(i + 1))
                    nc.vector.tensor_tensor(heads(ytmp), heads(k.ps[:, INT:INT + 2].rearrange("p a b -> p (a b)")),
                                            bc(v.eac[:, t, d * 16:d * 16 + 16], [P, HEADS, HEAD_DIM]), ALU.mult) \
                        .then_inc(k.inter_read.sem, 1)
                    dve.drain()
                    nc.vector.tensor_tensor(ysum, ysum, ytmp, ALU.add)
            gate(NT - 1)
    n = len(units)
    for x in (k.dtab_ready, k.acum_ready, k.seg_ready, k.decay_ready, k.m_ready):
        x.advance(n)
    for x in (k.y_ready, k.y_read, k.gated, k.cb_ready, k.cb_masked):
        x.advance(NT)
    k.group_summed.advance(n - NT)
    k.xd_ready.advance(2 * NT)
    for x in (k.inter_ready, k.inter_read):
        x.advance(len(inters))


def layer_norm(k, dve, row, stats, g_row, b_row, n):
    nc = k.nc
    dve.drain()
    nc.vector.bn_stats(stats[:, 0:6], row[:, 0:512])
    nc.vector.bn_stats(stats[:, 6:12], row[:, 512:1024])
    dve.drain()
    nc.vector.bn_aggr(stats[:, 12:14], stats[:, 0:12]).then_inc(k.var_ready.sem, 1)
    dve.drain()
    nc.vector.scalar_tensor_tensor(row, row, stats[:, 12:13], g_row, ALU.subtract, ALU.mult)
    dve.wait_ge(k.std_ready.sem, k.std_ready.at(n + 1))
    nc.vector.reciprocal(stats[:, 15:16], stats[:, 14:15])
    dve.drain()
    nc.vector.scalar_tensor_tensor(row, row, stats[:, 15:16], b_row, ALU.mult, ALU.add)


def norm_root(k, act, stats, n):
    act.wait_ge(k.var_ready.sem, k.var_ready.at(n + 1))
    k.nc.scalar.activation(stats[:, 14:15], stats[:, 13:14], ACT.Sqrt, bias=k.eps[:]).then_inc(k.std_ready.sem, 1)


def stage_merge(k, layer, stream, w0):
    nc, io = k.nc, k.io
    T = SEQ if stream == 0 else CTX_LEN
    NT, tb = T // P, (2 if stream == 0 else 0)
    grid = stream == 0
    ROWS, COLS = (SEQ // GRID_W, GRID_W) if grid else (1, CTX_LEN)
    v = mixer_views(k)
    s = v.scr
    ld = k.loaded.base
    pool_w = s[:, 0:1024].rearrange("p (g c) -> p g c", g=4)
    icnt = s[:, 1024:1024 + 2048].rearrange("p (g c) -> p g c", g=4)[:, :, 0:T]
    sig = s[:, 3072:3072 + 1024].rearrange("p (a b) -> p a b", a=2)
    g1row, lng, lnb = (s[:, 4096 + i * D:4096 + (i + 1) * D] for i in range(3))
    stats = s[:, 7168:7168 + 16]
    rms = s[:, 7200:7216].rearrange("p (t g) -> p t g", g=4)
    rinv = s[:, 7216:7232].rearrange("p (t g) -> p t g", g=4)
    SW = COLS + 2 * PAD
    pa = k.arena[:, 8192:8192 + ROWS * SW].rearrange("p (r c) -> p r c", r=ROWS)
    pb = k.arena[:, 8192 + 640:8192 + 640 + ROWS * SW].rearrange("p (r c) -> p r c", r=ROWS)
    ra = k.arena[:, 10240:10240 + 1536].rearrange("p (r c) -> p r c", r=24)
    rb = k.arena[:, 12288:12288 + 1536].rearrange("p (r c) -> p r c", r=24)
    tmp = k.arena[:, 12288 + 1536:12288 + 2048]
    sgs = k.arena[:, A_HIN:A_HIN + 4096].rearrange("p (m c) -> p m c", m=8)
    merged = k.arena[:, A_BT:A_BT + 4096].rearrange("p (m c) -> p m c", m=8)
    mixed = k.arena[:, A_TMP:A_TMP + 2048].rearrange("p (g c) -> p g c", g=4)
    hT = lambda kt, cut=slice(0, T): (k.act_a[:, kt, cut], k.act_b[:, kt, cut])
    yT = hT
    mT = lambda kt, cut: (k.act_c[:, kt, cut], k.act_e[:, kt, cut])
    cols = lambda w, m: (lambda kt: tuple(part[:, kt, (m % 2) * P:(m % 2 + 1) * P] for part in w))
    n_wide = 18
    mods = io["mods"][layer, stream]

    with nc.Block() as block:
        @block.sync
        def _(sp):
            sp.dma_start(pool_w, io["pool_w"][layer]).then_inc(k.loaded.sem, 16)
            ic = (io["icnt_grid"] if grid else io["icnt_line"])
            sp.dma_start(icnt, ic.unsqueeze(0).to_broadcast([P, 4, T])).then_inc(k.loaded.sem, 16)
            for dst, src in ((g1row, mods[2 * D:3 * D]), (lng, io["ln_g"][layer, 0]), (lnb, io["ln_b"][layer, 0])):
                sp.dma_start(dst, src.unsqueeze(0).to_broadcast([P, D])).then_inc(k.loaded.sem, 16)
            load_wides(k, sp, w0 + n_wide + WIDE_SLOTS)
            sp.wait_ge(k.loaded.sem, ld + 80)

        @block.tensor
        def _(pe):
            turn_tokens(k, pe, NT, tb)
            pe.wait_ge(k.h_hi.sem, k.h_hi.at(KT))
            for g in range(4):
                w = take_wide(k, pe, w0 + g // 2)
                if g >= 2:
                    pe.wait_ge(k.pin_copied.sem, k.pin_copied.at(g - 1))
                product(nc, k.ps[:, g % 2, 0:T], cols(w, g), hT,
                        ready=(lambda kt: pe.wait_ge(k.h_ready.sem, k.h_ready.at(kt + 1))) if g == 0 else None) \
                    .then_inc(k.pin_proj.sem, 1)
                if g % 2 == 1:
                    pe.drain().then_inc(k.wide_used.sem, 1)
            pe.wait_ge(k.pin_copied.sem, k.pin_copied.at(4))
            for m in range(8):
                w = take_wide(k, pe, w0 + 2 + m // 2)
                if m >= 2:
                    pe.wait_ge(k.gs_sig.sem, k.gs_sig.at(m - 1))
                product(nc, k.ps[:, m % 2, 0:T], cols(w, m), hT).then_inc(k.gs_proj.sem, 1)
                if m % 2 == 1:
                    pe.drain().then_inc(k.wide_used.sem, 1)
            pe.wait_ge(k.loaded.sem, ld + 80)
            for m in range(8):
                w = take_wide(k, pe, w0 + 6 + m // 2)
                if m >= 2:
                    pe.wait_ge(k.merged0.sem, k.merged0.at(m - 1))
                product(nc, k.ps[:, 2 + m % 2, 0:T], cols(w, m), hT).then_inc(k.gp_proj.sem, 1)
                if m % 2 == 1:
                    pe.drain().then_inc(k.wide_used.sem, 1)
                pe.wait_ge(k.mixed_ready.sem, k.mixed_ready.at(m // 2 + 1))
                nc.tensor.matmul(k.ps[:, 4 + m % 2, 0:T], pool_w[:, m // 2, (m % 2) * P:(m % 2 + 1) * P],
                                 mixed[:, m // 2, 0:T], start=True, stop=True).then_inc(k.yp_proj.sem, 1)
            for kt in range(KT):
                pe.wait_ge(k.yn_ready.sem, k.yn_ready.at(NT))
                if kt >= 2:
                    pe.wait_ge(k.yt_copied.sem, k.yt_copied.at(kt - 1))
                for t in range(NT):
                    last = nc.tensor.transpose(k.ps[:, 6 + kt % 2, t * P:(t + 1) * P],
                                               v.zs[:, t, kt * P:(kt + 1) * P], k.ident[:])
                last.then_inc(k.yt_turned.sem, 1)
            pe.wait_ge(k.yt_copied.sem, k.yt_copied.at(KT))
            pe.wait_ge(k.merged0.sem, k.merged0.at(8))
            for m in range(8):
                w = take_wide(k, pe, w0 + 10 + m // 2)
                if m >= 2:
                    pe.wait_ge(k.merged1.sem, k.merged1.at(m - 1))
                product(nc, k.ps[:, 2 + m % 2, 0:T], cols(w, m), yT).then_inc(k.ys_proj.sem, 1)
                if m % 2 == 1:
                    pe.drain().then_inc(k.wide_used.sem, 1)
            pe.wait_ge(k.gs_sig.sem, k.gs_sig.at(8))
            for n in range(4 * NT):
                w = take_wide(k, pe, w0 + 14 + n // NT)
                if n >= 2:
                    pe.wait_ge(k.mix_read.sem, k.mix_read.at(n - 1))
                t = n % NT
                product(nc, k.ps[:, n % 2, 0:WIDE], lambda kt: mT(kt, slice(t * P, (t + 1) * P)),
                        lambda kt: tuple(part[:, kt] for part in w),
                        ready=(lambda kt: pe.wait_ge(k.merged_lo.sem, k.merged_lo.at(kt + 1))) if n == 0 else None) \
                    .then_inc(k.mix_proj.sem, 1)
                if t == NT - 1:
                    pe.drain().then_inc(k.wide_used.sem, 1)

        @block.scalar
        def _(act):
            nc.scalar.activation(rms[:, 0:NT], v.e32[:, 0:NT, 0:GROUPS], ACT.Sqrt, bias=k.eps[:],
                                 scale=1.0 / GW).then_inc(k.rms_ready.sem, 1)
            round_wides(k, act, w0)
            modulate(k, act, v, T)
            round_wides(k, act, w0 + 1)
            for g in range(4):
                if g == 2:
                    round_wides(k, act, w0 + 2)
                act.wait_ge(k.pin_proj.sem, k.pin_proj.at(g + 1))
                nc.scalar.copy(mixed[:, g, 0:T], k.ps[:, g % 2, 0:T]).then_inc(k.pin_copied.sem, 1)
            for m in range(8):
                if m % 2 == 0:
                    round_wides(k, act, w0 + 2 + m // 2 + 1)
                act.wait_ge(k.gs_proj.sem, k.gs_proj.at(m + 1))
                nc.scalar.activation(sgs[:, m, 0:T], k.ps[:, m % 2, 0:T], ACT.Sigmoid).then_inc(k.gs_sig.sem, 1)
            for m in range(8):
                if m % 2 == 0:
                    round_wides(k, act, w0 + 6 + m // 2 + 1)
                act.wait_ge(k.gp_proj.sem, k.gp_proj.at(m + 1))
                if m >= 2:
                    act.wait_ge(k.merged0.sem, k.merged0.at(m - 1))
                nc.scalar.activation(sig[:, m % 2, 0:T], k.ps[:, 2 + m % 2, 0:T], ACT.Sigmoid) \
                    .then_inc(k.gp_sig.sem, 1)
            for kt in range(KT):
                act.wait_ge(k.yt_turned.sem, k.yt_turned.at(kt + 1))
                nc.scalar.activation(k.act_a[:, kt, 0:T], k.ps[:, 6 + kt % 2, 0:T], ACT.Copy,
                                     scale=v.pcols[:, PC_NORM + kt:PC_NORM + kt + 1]).then_inc(k.y_hi.sem, 1)
            for m in range(8):
                if m % 2 == 0:
                    round_wides(k, act, w0 + 10 + m // 2 + 1)
                act.wait_ge(k.merged1.sem, k.merged1.at(m + 1))
                nc.scalar.copy(k.act_c[:, m, 0:T], merged[:, m, 0:T]).then_inc(k.merged_hi.sem, 1)
            round_wides(k, act, w0 + n_wide)
            for t in range(NT):
                norm_root(k, act, stats, t)
                if t == 1:
                    round_wides(k, act, w0 + n_wide + 1)

        @block.gpsimd
        def _(pool):
            cut_wides(k, pool, w0 + n_wide + 1)

        @block.vector
        def _(dve):
            nc.vector.memset(pa, 0.0)
            nc.vector.memset(ra, 0.0)
            nc.vector.memset(rb, 0.0)
            modulate_rest(k, dve, v, k.act_b, T)
            dve.wait_ge(k.rms_ready.sem, k.rms_ready.at(1))
            nc.vector.reciprocal(rinv[:, 0:NT], rms[:, 0:NT])
            dve.drain()
            for t in range(NT):
                y = v.zs[:, t].rearrange("p (g c) -> p g c", g=GROUPS)
                nc.vector.tensor_tensor(y, y, bc(rinv[:, t], [P, GROUPS, GW]), ALU.mult).then_inc(k.yn_ready.sem, 1)
            dve.wait_ge(k.loaded.sem, ld + 80)
            for g, win in enumerate(POOL_WINDOWS):
                dve.wait_ge(k.pin_copied.sem, k.pin_copied.at(g + 1))
                grouped = mixed[:, g, 0:T].rearrange("p (r c) -> p r c", r=ROWS)
                dve.drain()
                nc.vector.tensor_copy(pa[:, :, PAD:PAD + COLS], grouped)
                dve.drain()
                src, dst, lo, hi, left, right = pa, pb, 1, SW, 1, 0
                w = 2
                while True:
                    n = hi - lo
                    nc.vector.tensor_tensor(dst[:, :, lo:hi], src[:, :, lo - left:lo - left + n],
                                            src[:, :, lo + right:lo + right + n], ALU.add)
                    dve.drain()
                    src, dst = dst, (pa if dst is pb else pb)
                    if w == win:
                        break
                    left = right = w // 2
                    lo, hi = lo + left, hi - right
                    w *= 2
                box = src[:, :, PAD:PAD + COLS]
                if grid:
                    nc.vector.tensor_copy(ra[:, PAD:PAD + ROWS], box)
                    dve.drain()
                    src, dst, lo, hi, left, right = ra, rb, 1, ROWS + 2 * PAD, 1, 0
                    w = 2
                    while True:
                        n = hi - lo
                        nc.vector.tensor_tensor(dst[:, lo:hi], src[:, lo - left:lo - left + n],
                                                src[:, lo + right:lo + right + n], ALU.add)
                        dve.drain()
                        src, dst = dst, src
                        if w == win:
                            break
                        left = right = w // 2
                        lo, hi = lo + left, hi - right
                        w *= 2
                    box = src[:, PAD:PAD + ROWS]
                rows = lambda ap: ap.rearrange("p (r c) -> p r c", r=ROWS)
                nc.vector.tensor_tensor(rows(tmp[:, 0:T]), box, rows(icnt[:, g]), ALU.mult)
                dve.drain()
                if grid and g < 3:
                    nc.vector.memset(ra, 0.0)
                    nc.vector.memset(rb, 0.0)
                nc.vector.memset(pa, 0.0)
                nc.vector.tensor_tensor(mixed[:, g, 0:T], tmp[:, 0:T], mixed[:, g, 0:T], ALU.subtract) \
                    .then_inc(k.mixed_ready.sem, 1)
            dve.drain()
            for m in range(8):
                dve.wait_ge(k.yp_proj.sem, k.yp_proj.at(m + 1))
                dve.wait_ge(k.gp_sig.sem, k.gp_sig.at(m + 1))
                nc.vector.scalar_tensor_tensor(merged[:, m, 0:T], k.ps[:, 4 + m % 2, 0:T],
                                               v.pcols[:, PC_SCALE + m:PC_SCALE + m + 1], sig[:, m % 2, 0:T],
                                               ALU.mult, ALU.mult).then_inc(k.merged0.sem, 1)
            for kt in range(KT):
                dve.wait_ge(k.y_hi.sem, k.y_hi.at(kt + 1))
                nc.vector.scalar_tensor_tensor(k.act_b[:, kt, 0:T], k.ps[:, 6 + kt % 2, 0:T],
                                               v.pcols[:, PC_NORM + kt:PC_NORM + kt + 1],
                                               k.act_a[:, kt, 0:T].bitcast(F32), ALU.mult, ALU.subtract) \
                    .then_inc(k.yt_copied.sem, 1)
            dve.wait_ge(k.gs_sig.sem, k.gs_sig.at(8))

            def merged_rest(m):
                dve.wait_ge(k.merged_hi.sem, k.merged_hi.at(m + 1))
                nc.vector.tensor_tensor(k.act_e[:, m, 0:T], merged[:, m, 0:T], k.act_c[:, m, 0:T].bitcast(F32),
                                        ALU.subtract).then_inc(k.merged_lo.sem, 1)

            for m in range(8):
                dve.wait_ge(k.ys_proj.sem, k.ys_proj.at(m + 1))
                dve.drain()
                nc.vector.tensor_tensor(tmp[:, 0:T], k.ps[:, 2 + m % 2, 0:T], sgs[:, m, 0:T], ALU.mult)
                dve.drain()
                nc.vector.tensor_tensor(merged[:, m, 0:T], merged[:, m, 0:T], tmp[:, 0:T], ALU.add) \
                    .then_inc(k.merged1.sem, 1)
                if m >= 1:
                    merged_rest(m - 1)
            merged_rest(7)
            for n in range(4 * NT):
                t, quarter = n % NT, slice((n // NT) * WIDE, (n // NT + 1) * WIDE)
                dve.wait_ge(k.mix_proj.sem, k.mix_proj.at(n + 1))
                dve.drain()
                nc.vector.tensor_tensor(tmp[:, 0:WIDE], k.ps[:, n % 2, 0:WIDE], g1row[:, quarter], ALU.mult).then_inc(k.mix_read.sem, 1)
                dve.drain()
                x = k.res[:, tb + t, quarter]
                nc.vector.scalar_tensor_tensor(x, x, ALPHA, tmp[:, 0:WIDE], ALU.mult, ALU.add)
                if n >= 3 * NT:
                    layer_norm(k, dve, k.res[:, tb + t], stats, lng, lnb, t)
    k.loaded.advance(80)
    k.rms_ready.advance(1)
    for x in (k.pin_copied, k.mixed_ready, k.pin_proj):
        x.advance(4)
    for x in (k.gp_proj, k.gp_sig, k.yp_proj, k.merged0, k.gs_proj, k.gs_sig, k.ys_proj, k.merged1,
              k.yt_turned, k.yt_copied, k.y_hi, k.merged_hi, k.merged_lo, k.xt_ready, k.h_hi, k.h_ready):
        x.advance(8)
    for x in (k.mix_proj, k.mix_read):
        x.advance(4 * NT)
    for x in (k.var_ready, k.std_ready, k.yn_ready):
        x.advance(NT)
    return w0 + n_wide


def peer_views(k, NT):
    v = Bag()
    ring, h2, scores, dg, small = carve(k, RING * 2 * D, 4 * D, 4 * 2048 + 256, 8 * P, 2000)
    v.ring = ring.rearrange("p (s c) -> p s c", s=RING)
    v.raw_ring = ring
    v.h2 = h2.rearrange("p (t c) -> p t c", t=4)
    v.scores, v.g2, v.lng, v.lnb = scores, k.rows[:, 0], k.rows[:, 1], k.rows[:, 2]
    v.diag = dg.rearrange("p (s c) -> p s c", s=8)
    v.small = small
    return v


def chooser(k, layer, v):
    nc = k.nc
    at = [0]

    def small(n, dt=F32):
        a = v.small[:, at[0]:at[0] + n]
        at[0] += n
        return a if dt == F32 else a.bitcast(dt)

    sc, sc2 = small(256), small(256)
    sv, si, sif = small(32), small(32, U32), small(32)
    cand, cand2 = small(256), small(256)
    tv, tp = small(16), small(16, U32)
    ab, abf, hot, pair = small(32, U32), small(32), small(512), small(32)
    nmax, esum, einv = small(1), small(1), small(1)
    idf = small(16)
    idx, gate = small(32, U32), small(32)
    act_in, gel, wgt = small(32), small(32), small(32)
    stats = small(16)

    def top16(dve, val, ind, src, spare):
        nc.vector.max(val[:, 0:8], src)
        dve.drain()
        nc.vector.max_index(ind[:, 0:8], val[:, 0:8], src)
        nc.vector.match_replace(spare, val[:, 0:8], src, NEG)
        dve.drain()
        nc.vector.max(val[:, 8:16], spare)
        dve.drain()
        nc.vector.max_index(ind[:, 8:16], val[:, 8:16], spare)

    def choose_a(dve, score_ap):
        nc.vector.tensor_copy(sc, score_ap)
        dve.drain()
        for half in range(2):
            top16(dve, sv[:, half * 16:half * 16 + 16], si[:, half * 16:half * 16 + 16],
                  sc[:, half * P:(half + 1) * P], sc2[:, half * P:(half + 1) * P])
        dve.drain()
        nc.vector.tensor_copy(sif, si)

    def choose_b(dve, par, unit):
        c3 = cand.rearrange("p (a b) -> p a b", a=TOPK)
        nc.vector.tensor_tensor(c3, bc(sv[:, 0:16], [P, TOPK, TOPK]),
                                sv[:, 16:32].unsqueeze(1).to_broadcast([P, TOPK, TOPK]), ALU.add)
        dve.drain()
        top16(dve, tv, tp, cand, cand2)
        nc.vector.tensor_scalar(nmax, tv[:, 0:1], -1.0, None, ALU.mult).then_inc(k.top_ready.sem, 1)
        dve.drain()
        nc.vector.tensor_scalar(ab[:, 0:16], tp, 4, None, ALU.logical_shift_right)
        nc.vector.tensor_scalar(ab[:, 16:32], tp, 15, None, ALU.bitwise_and)
        dve.drain()
        nc.vector.tensor_copy(abf, ab)
        dve.drain()
        h3 = hot.rearrange("p (s b) -> p s b", b=TOPK)
        nc.vector.tensor_tensor(h3, bc(abf, [P, 32, TOPK]), k.iota[:].unsqueeze(1).to_broadcast([P, 32, TOPK]),
                                ALU.is_equal)
        dve.drain()
        h4 = hot.rearrange("p (z s b) -> p z s b", z=2, b=TOPK)
        s4 = sif.rearrange("p (z b) -> p z b", z=2).unsqueeze(2).to_broadcast([P, 2, TOPK, TOPK])
        nc.vector.tensor_tensor(h4, h4, s4, ALU.mult)
        dve.drain()
        nc.vector.tensor_reduce(pair, h3, AX_X, ALU.add)
        dve.drain()
        nc.vector.scalar_tensor_tensor(idf, pair[:, 0:16], float(N_KEYS), pair[:, 16:32], ALU.mult, ALU.add)
        dve.drain()
        nc.vector.tensor_scalar(idx[:, par * 16:par * 16 + 16], idf, float(layer * N_EXPERTS), None, ALU.add) \
            .then_inc(k.idx_ready.sem, 1)
        dve.wait_ge(k.soft_done.sem, unit + 1)
        nc.vector.reciprocal(einv, esum)
        dve.drain()
        g = gate[:, par * 16:par * 16 + 16]
        nc.vector.tensor_scalar(g, g, einv, None, ALU.mult)

    def softmax(act, par, unit):
        act.wait_ge(k.top_ready.sem, unit + 1)
        nc.scalar.activation(gate[:, par * 16:par * 16 + 16], tv, ACT.Exp, bias=nmax,
                             accum_out=esum).then_inc(k.soft_done.sem, 1)

    c = Bag()
    c.idx, c.gate, c.act_in, c.gel, c.wgt, c.stats = idx, gate, act_in, gel, wgt, stats
    c.choose_a, c.choose_b, c.softmax = choose_a, choose_b, softmax
    return c


def stage_queries(k, layer, stream, w0):
    nc, io = k.nc, k.io
    T = SEQ if stream == 0 else CTX_LEN
    NT, tb = T // P, (2 if stream == 0 else 0)
    v = peer_views(k, NT)
    ld = k.loaded.base
    mods = io["mods"][layer, stream]
    h2T = lambda kt: (k.act_a[:, kt, 0:T], k.act_b[:, kt, 0:T])
    keys = v.raw_ring[:, 8192:10240].rearrange("p (a b) -> p a b", a=16)
    qT = v.raw_ring[:, 10240:11264].rearrange("p (a b) -> p a b", a=2)
    sh2, sc2 = v.raw_ring[:, 11264:12288], v.raw_ring[:, 12288:13312]
    n_wide = 8
    M = 2 * PEER_HEADS
    c, u0 = chooser(k, layer, v), k.idx_ready.base
    CHOOSE_A, CHOOSE_B, SOFTMAX = 3, 8, 10

    with nc.Block() as block:
        @block.sync
        def _(sp):
            for dst, src in ((sh2, mods[3 * D:4 * D]), (sc2, mods[4 * D:5 * D])):
                sp.dma_start(dst, src.unsqueeze(0).to_broadcast([P, D])).then_inc(k.loaded.sem, 16)
            sp.dma_start(keys, io["keys"][layer]).then_inc(k.loaded.sem, 16)
            load_wides(k, sp, w0 + n_wide + WIDE_SLOTS)
            sp.wait_ge(k.loaded.sem, ld + 48)

        @block.vector
        def _(dve):
            nc.vector.memset(v.scores[:, NT * 2048:NT * 2048 + 256], 0.0)
            dve.wait_ge(k.loaded.sem, ld + 48)
            for t in range(NT):
                nc.vector.scalar_tensor_tensor(v.h2[:, t], sc2, 1.0, k.res[:, tb + t], ALU.add, ALU.mult)
                dve.drain()
                nc.vector.tensor_tensor(v.h2[:, t], v.h2[:, t], sh2, ALU.add).then_inc(k.h2_ready.sem, 1)
            for kt in range(KT):
                dve.wait_ge(k.h2_hi.sem, k.h2_hi.at(kt + 1))
                nc.vector.tensor_tensor(k.act_b[:, kt, 0:T], k.ps[:, kt % 2, 0:T], k.act_a[:, kt, 0:T].bitcast(F32),
                                        ALU.subtract).then_inc(k.h2_copied.sem, 1)
            for m in range(M):
                dve.wait_ge(k.s_proj.sem, k.s_proj.at(m + 1))
                dst = v.scores[:, 0:NT * 2048].rearrange("p (t c) -> p t c", t=NT)[:, :, m * P:(m + 1) * P]
                nc.vector.tensor_copy(dst, k.ps[:, 4 + m % 2, 0:T].rearrange("p (t c) -> p t c", c=P)) \
                    .then_inc(k.s_copied.sem, 1)
                if m == CHOOSE_A:
                    dve.drain()
                    c.choose_a(dve, v.scores[:, 0:256])
                if m == CHOOSE_B:
                    dve.drain()
                    c.choose_b(dve, 0, u0)

        @block.scalar
        def _(act):
            round_wides(k, act, w0)
            for kt in range(KT):
                act.wait_ge(k.h2_turned.sem, k.h2_turned.at(kt + 1))
                nc.scalar.copy(k.act_a[:, kt, 0:T], k.ps[:, kt % 2, 0:T]).then_inc(k.h2_hi.sem, 1)
            round_wides(k, act, w0 + 1)
            for m in range(M):
                if m % 2 == 0 and 2 <= m and m // 2 + 1 < n_wide:
                    round_wides(k, act, w0 + m // 2 + 1)
                act.wait_ge(k.q_proj.sem, k.q_proj.at(m + 1))
                if m >= 2:
                    act.wait_ge(k.s_proj.sem, k.s_proj.at(m - 1))
                nc.scalar.copy(qT[:, m % 2, 0:T], k.ps[:, 2 + m % 2, 0:T]).then_inc(k.q_copied.sem, 1)
                if m == SOFTMAX:
                    c.softmax(act, 0, u0)

        @block.gpsimd
        def _(pool):
            cut_wides(k, pool, w0 + n_wide - 1)

        @block.tensor
        def _(pe):
            pe.wait_ge(k.h2_ready.sem, k.h2_ready.at(NT))
            for kt in range(KT):
                if kt >= 2:
                    pe.wait_ge(k.h2_copied.sem, k.h2_copied.at(kt - 1))
                for t in range(NT):
                    last = nc.tensor.transpose(k.ps[:, kt % 2, t * P:(t + 1) * P], v.h2[:, t, kt * P:(kt + 1) * P],
                                               k.ident[:])
                last.then_inc(k.h2_turned.sem, 1)
            pe.wait_ge(k.loaded.sem, ld + 48)

            def score(m):
                pe.wait_ge(k.q_copied.sem, k.q_copied.at(m + 1))
                if m >= 2:
                    pe.wait_ge(k.s_copied.sem, k.s_copied.at(m - 1))
                for t in range(NT):
                    last = nc.tensor.matmul(k.ps[:, 4 + m % 2, t * P:(t + 1) * P], qT[:, m % 2, t * P:(t + 1) * P],
                                            keys[:, m], start=True, stop=True)
                last.then_inc(k.s_proj.sem, 1)

            for m in range(M):
                wh, wl = take_wide(k, pe, w0 + m // 2)
                cut = slice((m % 2) * P, (m % 2 + 1) * P)
                if m >= 2:
                    pe.wait_ge(k.q_copied.sem, k.q_copied.at(m - 1))
                product(nc, k.ps[:, 2 + m % 2, 0:T], lambda kt: (wh[:, kt, cut], wl[:, kt, cut]), h2T,
                        ready=(lambda kt: pe.wait_ge(k.h2_copied.sem, k.h2_copied.at(kt + 1))) if m == 0 else None) \
                    .then_inc(k.q_proj.sem, 1)
                if m % 2 == 1:
                    pe.drain().then_inc(k.wide_used.sem, 1)
                if m >= 1:
                    score(m - 1)
            score(M - 1)
    k.loaded.advance(48)
    k.h2_ready.advance(NT)
    for x in (k.h2_turned, k.h2_hi, k.h2_copied):
        x.advance(KT)
    for x in (k.q_proj, k.q_copied, k.s_proj, k.s_copied):
        x.advance(M)
    return w0 + n_wide


def stage_retrieve(k, layer, stream, last_stage):
    nc, io = k.nc, k.io
    T = SEQ if stream == 0 else CTX_LEN
    NT, tb = T // P, (2 if stream == 0 else 0)
    v = peer_views(k, NT)
    UNITS = NT * PEER_HEADS
    SEL = UNITS * TOPK
    ROUNDS = SEL // RING
    c = chooser(k, layer, v)
    idx, gate, act_in, gel, wgt, stats, softmax = c.idx, c.gate, c.act_in, c.gel, c.wgt, c.stats, c.softmax
    ld = k.loaded.base
    s0 = k.slot_free.base
    u0, r0, d0, q0 = (k.idx_ready.base, k.landed[0].base // 16, k.diags.base, k.dots.base)

    with nc.Block() as block:
        @block.gpsimd
        def _(pool):
            for t in range(NT):
                with pool.Fori(0, PEER_HEADS // 2) as i:
                    for par in range(2):
                        pool.wait_ge(k.idx_ready.sem, i * 2 + (u0 + t * 8 + par + 1))
                        pool.sem_inc(k.pool_steps.sem, 1)
                        for j in range(TOPK):
                            pool.wait_ge(k.slot_free.sem, i * 32 + (s0 + t * 128 + par * 16 + j + 1))
                            pool.sem_inc(k.pool_steps.sem, 1)
                            pool.indirect_dma_start(
                                out=v.ring[:, j % RING], out_offset=None, in_=io["experts"],
                                in_offset=bass.IndirectOffsetOnAxis(
                                    ap=idx[:, par * 16 + j:par * 16 + j + 1], axis=0),
                            ).then_inc(k.landed[j % RING].sem, 16)

        @block.vector
        def _(dve):
            def finish(t):
                dve.wait_ge(k.loaded.sem, ld + 48)
                dve.wait_ge(k.acc_ready.sem, k.acc_ready.at(t + 1))
                x = k.res[:, tb + t]
                a = 2 * (t % 2)
                wsum = v.h2[:, t]
                nc.vector.tensor_tensor(wsum, k.ps[:, a:a + 2].rearrange("p a b -> p (a b)"), v.g2, ALU.mult) \
                    .then_inc(k.acc_read.sem, 1)
                dve.drain()
                nc.vector.scalar_tensor_tensor(x, x, ALPHA, wsum, ALU.mult, ALU.add)
                layer_norm(k, dve, x, stats, v.lng, v.lnb, t)
                dve.drain().then_inc(k.stored.sem, 1)

            for t in range(NT):
                with dve.Fori(0, PEER_HEADS // 2) as i:
                    for par in range(2):
                        for q in range(TOPK // GRP):
                            for j in range(q * GRP, (q + 1) * GRP):
                                slot = j % RING
                                dve.wait_ge(k.landed[slot].sem,
                                            i * 64 + 16 * (r0 + t * 16 + par * 2 + j // RING + 1))
                                u_row = v.ring[:, slot, 0:D]
                                last = nc.vector.tensor_tensor_reduce(
                                    out=u_row, in0=u_row, in1=v.h2[:, t], scale=1.0, scalar=0.0,
                                    op0=ALU.mult, op1=ALU.add, accum_out=act_in[:, j:j + 1])
                            last.then_inc(k.dots.sem, 1)
                            dve.wait_ge(k.gelus.sem, i * 8 + (q0 + t * 32 + par * 4 + q + 1))
                            nc.vector.tensor_tensor(wgt[:, j - 3:j + 1], gel[:, j - 3:j + 1],
                                                    gate[:, par * 16 + j - 3:par * 16 + j + 1], ALU.mult) \
                                .then_inc(k.weights.sem, 1)
                            if q == 0:
                                c.choose_a(dve, v.scores[:, bass.ds(i * 512 + (t * 2048 + (par + 1) * 256), 256)])
                            if q == 1:
                                c.choose_b(dve, 1 - par, i * 2 + (u0 + t * 8 + par + 1))
                            dve.drain()
                if t >= 1:
                    finish(t - 1)
            finish(NT - 1)

        @block.scalar
        def _(act):
            for t in range(NT):
                with act.Fori(0, PEER_HEADS // 2) as i:
                    for par in range(2):
                        for q in range(TOPK // GRP):
                            n = i * 8 + (q0 + t * 32 + par * 4 + q + 1)
                            act.wait_ge(k.dots.sem, n)
                            nc.scalar.activation(gel[:, q * GRP:(q + 1) * GRP], act_in[:, q * GRP:(q + 1) * GRP],
                                                 ACT.Gelu_apprx_tanh).then_inc(k.gelus.sem, 1)
                            act.wait_ge(k.weights.sem, n)
                            for j in range(q * GRP, (q + 1) * GRP):
                                if j % GRP == 0:
                                    act.wait_ge(k.slot_free.sem,
                                                i * 32 + (s0 + t * 128 + par * 16 + j + GRP))
                                nc.scalar.activation(v.diag[:, j % 8], k.ident[:], ACT.Copy,
                                                     scale=wgt[:, j:j + 1]).then_inc(k.diags.sem, 1)
                            if q == 1:
                                softmax(act, 1 - par, i * 2 + (u0 + t * 8 + par + 1))
                if t >= 1:
                    norm_root(k, act, stats, t - 1)
            norm_root(k, act, stats, NT - 1)

        @block.tensor
        def _(pe):
            if s0 == 0:
                pe.sem_inc(k.slot_free.sem, RING)
            for t in range(NT):
                a = 2 * (t % 2)
                if t >= 2:
                    pe.wait_ge(k.acc_read.sem, k.acc_read.at(t - 1))
                for half in range(2):
                    nc.tensor.matmul(k.ps[:, a + half], k.zeros[:, 0:P], k.zeros[:], start=True, stop=False,
                                     skip_group_check=True)
                with pe.Fori(0, PEER_HEADS // 2) as i:
                    for j in range(2 * TOPK):
                        pe.wait_ge(k.diags.sem, i * 32 + (d0 + t * 128 + j + 1))
                        for half in range(2):
                            mm = nc.tensor.matmul(k.ps[:, a + half], v.diag[:, j % 8],
                                                  v.ring[:, j % RING, D + half * BANK:D + (half + 1) * BANK],
                                                  start=False, stop=False, skip_group_check=True)
                        mm.then_inc(k.slot_free.sem, 1)
                for half in range(2):
                    mm = nc.tensor.matmul(k.ps[:, a + half], k.zeros[:, 0:P], k.zeros[:], start=False, stop=True,
                                          skip_group_check=True)
                mm.then_inc(k.acc_ready.sem, 1)

        @block.sync
        def _(sp):
            mods = io["mods"][layer, stream]
            for n, src in enumerate((mods[5 * D:6 * D], io["ln_g"][layer, 1], io["ln_b"][layer, 1])):
                sp.dma_start(k.rows[:, n], src.unsqueeze(0).to_broadcast([P, D])).then_inc(k.loaded.sem, 16)
            sp.wait_ge(k.loaded.sem, ld + 48)
            if last_stage:
                for t in range(NT):
                    sp.wait_ge(k.stored.sem, k.stored.at(t + 1))
                    sp.dma_start(io["out"][t * P:(t + 1) * P], k.res[:, tb + t]).then_inc(k.mods_stored.sem, 16)
                sp.wait_ge(k.mods_stored.sem, 16 + 16 * NT)
    k.loaded.advance(48)
    k.slot_free.advance(SEL)
    for x in (k.idx_ready, k.top_ready, k.soft_done):
        x.advance(UNITS + 1)
    for x in k.landed:
        x.advance(16 * ROUNDS)
    k.dots.advance(SEL // GRP)
    k.gelus.advance(SEL // GRP)
    k.weights.advance(SEL // GRP)
    k.diags.advance(SEL)
    for x in (k.acc_ready, k.acc_read, k.var_ready, k.std_ready, k.stored):
        x.advance(NT)


LATENT, CONTEXT = 0, 1


def build(nc, io):
    with ExitStack() as ctx:
        k = setup(nc, ctx, io)
        plan = k.wide_plan
        for layer in range(DEPTH):
            plan += [(layer, W_MOD + b) for b in range(N_MOD)]
        for layer in range(DEPTH):
            for stream in (CONTEXT, LATENT):
                full = stream == LATENT or layer < DEPTH - 1
                order = [b for a, z in ((W_SCAN, W_GP), (W_GS, W_SSD), (W_GP, W_GS), (W_SSD, W_Q)) for b in range(a, z)]
                plan += [(layer, b) for b in (order if full else range(W_Z))]
            for stream in (CONTEXT, LATENT):
                if stream == LATENT or layer < DEPTH - 1:
                    plan += [(layer, W_Q + b) for b in range(W_MOD - W_Q)]
        w = stage_mods(k)
        for layer in range(DEPTH):
            last = layer == DEPTH - 1
            for stream in (CONTEXT, LATENT):
                full = stream == LATENT or not last
                w = stage_project(k, layer, stream, w, full)
                stage_states(k, stream)
                if full:
                    stage_outputs(k, stream)
                    w = stage_merge(k, layer, stream, w)
            for stream in (CONTEXT, LATENT):
                if stream == LATENT or not last:
                    w = stage_queries(k, layer, stream, w)
                    stage_retrieve(k, layer, stream, last and stream == LATENT)


def wide_blocks(w):
    n = w.shape[1] // WIDE
    return w.reshape(KT, P, n, WIDE).transpose(2, 1, 0, 3).reshape(n, P, KT * WIDE)


def inverse_counts(length, win):
    t = np.arange(length)
    lo, hi = np.maximum(t - win // 2, 0), np.minimum(t + win - 1 - win // 2, length - 1)
    return (1.0 / (hi - lo + 1)).astype(np.float32)


def kernel(x, c, ctx, c_ctx, w_mod, b_mod, w_in, conv_w, conv_b, a_log, dt_bias, d_skip,
           ssd_norm_g, w_ssd_out, pool_w, pool_scale, w_o, ln_g, ln_b, w_q, sub_keys, u_tab, v_tab):
    import concourse.bacc as bacc
    from concourse.bass_utils import run_bass_kernel_spmd

    A = np.asarray
    w_in = A(w_in)
    wide = np.empty((DEPTH, N_WIDE, P, KT * WIDE), np.float32)
    for l in range(DEPTH):
        wide[l, W_SCAN:W_Z] = wide_blocks(w_in[l, :, 0:COL_DT])
        wide[l, W_Z:W_SSD] = wide_blocks(w_in[l, :, COL_Z:])
        wide[l, W_SSD:W_O] = wide_blocks(A(w_ssd_out)[l])
        wide[l, W_O:W_Q] = wide_blocks(A(w_o)[l])
        wide[l, W_Q:W_MOD] = wide_blocks(A(w_q)[l])
        wide[l, W_MOD:] = wide_blocks(A(w_mod)[l])
    cols = lambda a: A(a).reshape(DEPTH, -1, P).transpose(0, 2, 1)
    taps = A(conv_w).reshape(DEPTH, CONV_W, SCAN_TILES, P).transpose(0, 3, 2, 1).reshape(DEPTH, P, -1)
    grid = [np.outer(inverse_counts(SEQ // GRID_W, w), inverse_counts(GRID_W, w)).reshape(-1) for w in POOL_WINDOWS]
    tri = np.triu(np.ones((P, P), np.float32))
    arrays = {
        "wide": wide,
        "w_dt": w_in[:, :, COL_DT:COL_Z].reshape(DEPTH, KT, P, 32).transpose(0, 2, 1, 3),
        "cvec": np.stack([A(c)[0], A(c_ctx)]).reshape(2, KT, P).transpose(2, 1, 0),
        "b_mod": A(b_mod)[None],
        "tokens": np.concatenate([A(ctx)[0], A(x)[0]]).reshape(6, P, D),
        "pcols": np.concatenate([taps, cols(conv_b), cols(pool_scale), cols(ssd_norm_g)], axis=2),
        "hrows": np.concatenate([A(a_log).reshape(DEPTH, 32), A(dt_bias).reshape(DEPTH, 32), A(d_skip)], axis=1),
        "pool_w": A(pool_w).transpose(0, 2, 1, 3),
        "ln_g": A(ln_g), "ln_b": A(ln_b),
        "keys": A(sub_keys).transpose(0, 4, 1, 2, 3).reshape(DEPTH, P, 16, N_KEYS),
        "experts": np.concatenate([A(u_tab), A(v_tab)], axis=2).reshape(DEPTH * N_EXPERTS, 2 * D),
        "ident": np.eye(P, dtype=np.float32),
        "tri": np.stack([tri, tri.T], axis=1),
        "iota": np.tile(np.arange(TOPK, dtype=np.float32), (P, 1)),
        "icnt_grid": np.stack(grid).astype(np.float32),
        "icnt_line": np.stack([inverse_counts(CTX_LEN, w) for w in POOL_WINDOWS]),
    }
    nc = bacc.Bacc("TRN2", target_bir_lowering=False, num_devices=1)
    io = {}
    for name, a in arrays.items():
        arrays[name] = np.ascontiguousarray(a)
        io[name] = nc.dram_tensor(f"in_{name}", a.shape, F32, kind="ExternalInput").ap()
    io["mods"] = nc.dram_tensor("mod_rows", (DEPTH, 2, 6 * D), F32, kind="Internal").ap()
    io["out"] = nc.dram_tensor("out_x", (SEQ, D), F32, kind="ExternalOutput").ap()
    build(nc, io)
    r = run_bass_kernel_spmd(nc, [{f"in_{n}": a for n, a in arrays.items()}], core_ids=[0])
    return r.results[0]["out_x"].reshape(1, SEQ, D)
```
